# Optimizing a Trainium2 kernel written in Bass

```python
import functools
import jax, jax.numpy as jnp
from jax import lax
import numpy as np

D_MODEL = 1024
BATCH = 1
SEQ = 1024
DEPTH = 2
DEC_BATCH = 8
DEC_SEQ = 4
PAST_LEN = 256
PAGE_SIZE = 128

N_META = 16
N_A_LAYERS = DEPTH // 2
N_B_LAYERS = DEPTH - N_A_LAYERS
CONV_WIDTH = 3
N_HEADS = 16
HEAD_DIM = D_MODEL // N_HEADS
ATTN_DIM = N_HEADS * HEAD_DIM
D_FF = 4 * D_MODEL
Q_BLOCK = 128
RMS_EPS = 1e-6
FORGET_BIAS = 3.0
NEG_INF = -1e30

kernel_name = "yoco_shortconv_fox_decoder_step"

def rms_norm(x, g):
    xf = x.astype(jnp.float32)
    y = xf * lax.rsqrt(jnp.mean(xf * xf, axis=-1, keepdims=True) + RMS_EPS)
    return (y * g.astype(jnp.float32)).astype(x.dtype)

def squared_relu_mlp(xn, w1, w2):
    return jnp.square(jax.nn.relu(xn @ w1)) @ w2

def short_conv_mixer(xn, conv_state, w_in, conv_w, w_out):
    T = xn.shape[1]
    b, c, h = jnp.split(xn @ w_in, 3, axis=-1)
    u = c * h
    u_pad = jnp.concatenate([conv_state.astype(u.dtype), u], axis=1)
    conv = conv_w[CONV_WIDTH - 1] * u_pad[:, CONV_WIDTH - 1:]
    for j in range(CONV_WIDTH - 1):
        conv = conv + conv_w[j] * u_pad[:, j:j + T]
    y = (b * conv) @ w_out
    return y, u_pad[:, T:]

def shared_kv(h, norm_kv, w_kv, k_norm, w_f, b_f):
    N, T, _ = h.shape
    xn = rms_norm(h, norm_kv)
    k, v = jnp.split(xn @ w_kv, 2, axis=-1)
    k = rms_norm(k.reshape(N, T, N_HEADS, HEAD_DIM), k_norm)
    v = v.reshape(N, T, N_HEADS, HEAD_DIM)
    logf = jax.nn.log_sigmoid((xn @ w_f + b_f).astype(jnp.float32)).astype(h.dtype)
    return k, v, logf

def forget_attention(q, k, v, c_q, c_k, q_pos, k_pos):
    s = jnp.einsum('nqhd,nkhd->nhqk', q, k, preferred_element_type=jnp.float32) * (HEAD_DIM ** -0.5)
    s = s + (jnp.transpose(c_q, (0, 2, 1))[:, :, :, None] - jnp.transpose(c_k, (0, 2, 1))[:, :, None, :])
    causal = k_pos[None, :] <= q_pos[:, None]
    s = jnp.where(causal[None, None], s, NEG_INF)
    p = jax.nn.softmax(s, axis=-1)
    return jnp.einsum('nhqk,nkhd->nqhd', p.astype(v.dtype), v)

def prompt_prepare(k, v, logf):
    T = k.shape[1]
    pad = (-T) % Q_BLOCK
    k = jnp.pad(k, ((0, 0), (0, pad), (0, 0), (0, 0)))
    v = jnp.pad(v, ((0, 0), (0, pad), (0, 0), (0, 0)))
    c = jnp.cumsum(jnp.pad(logf.astype(jnp.float32), ((0, 0), (0, pad), (0, 0))), axis=1)
    return k, v, c

def prompt_attend(q, ctx):
    k, v, c = ctx
    N, T = q.shape[:2]
    Tp = k.shape[1]
    nb = Tp // Q_BLOCK
    qp = jnp.pad(q, ((0, 0), (0, Tp - T), (0, 0), (0, 0)))
    pos = jnp.arange(Tp, dtype=jnp.int32)
    qb = qp.reshape(N, nb, Q_BLOCK, N_HEADS, HEAD_DIM).swapaxes(0, 1)
    cb = c.reshape(N, nb, Q_BLOCK, N_HEADS).swapaxes(0, 1)
    pb = pos.reshape(nb, Q_BLOCK)

    def block(args):
        q_blk, c_blk, p_blk = args
        return forget_attention(q_blk, k, v, c_blk, c, p_blk, pos)

    out = lax.map(block, (qb, cb, pb))
    return out.swapaxes(0, 1).reshape(N, Tp, N_HEADS, HEAD_DIM)[:, :T]

def gather_pages(cache, page_table):
    g = cache[page_table]
    return g.reshape((page_table.shape[0], page_table.shape[1] * cache.shape[1]) + cache.shape[2:])

def sample_prepare(k, v, logf, past_k, past_v, past_logf):
    k_all = jnp.concatenate([past_k.astype(k.dtype), k], axis=1)
    v_all = jnp.concatenate([past_v.astype(v.dtype), v], axis=1)
    c_all = jnp.cumsum(jnp.concatenate([past_logf.astype(jnp.float32), logf.astype(jnp.float32)], axis=1), axis=1)
    return k_all, v_all, c_all

def sample_attend(q, ctx):
    k_all, v_all, c_all = ctx
    L = k_all.shape[1]
    Tq = q.shape[1]
    pos = jnp.arange(L, dtype=jnp.int32)
    return forget_attention(q, k_all, v_all, c_all[:, L - Tq:], c_all, pos[L - Tq:], pos)

def decoder_trunk(x, conv_state, prepare, attend, norm_mix, norm_mlp, conv_w_in, conv_w, conv_w_out,
                  norm_kv, w_kv, k_norm, w_f, b_f, w_q, q_norm, w_o, mlp_w1, mlp_w2):
    N, T, _ = x.shape
    conv_rows = []
    for layer in range(DEPTH):
        xn = rms_norm(x, norm_mix[layer])
        if layer < N_A_LAYERS:
            y, st = short_conv_mixer(xn, conv_state[layer], conv_w_in[layer], conv_w[layer], conv_w_out[layer])
            conv_rows.append(st)
        else:
            j = layer - N_A_LAYERS
            if j == 0:
                k, v, logf = shared_kv(x, norm_kv, w_kv, k_norm, w_f, b_f)
                ctx = prepare(k, v, logf)
            q = rms_norm((xn @ w_q[j]).reshape(N, T, N_HEADS, HEAD_DIM), q_norm[j])
            y = attend(q, ctx).reshape(N, T, ATTN_DIM) @ w_o[j]
        x = x + y
        x = x + squared_relu_mlp(rms_norm(x, norm_mlp[layer]), mlp_w1[layer], mlp_w2[layer])
    return x, jnp.stack(conv_rows), k, v, logf

def setup_inputs(seed: int = 0) -> dict:
    key = jax.random.key(seed)
    ks = jax.random.split(key, 26)
    f32 = jnp.float32
    n_pages = PAST_LEN // PAGE_SIZE
    n_used = DEC_BATCH * n_pages
    n_pool = (5 * n_used + 3) // 4

    def nrm(k, shape, scale):
        return scale * jax.random.normal(k, shape, f32)

    return {
        "x_prompt": nrm(ks[0], (BATCH, SEQ, D_MODEL), 1.0),
        "x_sample": nrm(ks[1], (DEC_BATCH, DEC_SEQ, D_MODEL), 1.0),
        "cache_k": nrm(ks[2], (n_pool, PAGE_SIZE, N_HEADS, HEAD_DIM), 1.0),
        "cache_v": nrm(ks[3], (n_pool, PAGE_SIZE, N_HEADS, HEAD_DIM), 1.0),
        "cache_logf": jax.nn.log_sigmoid(FORGET_BIAS + nrm(ks[4], (n_pool, PAGE_SIZE, N_HEADS), 1.0)),
        "state_conv": nrm(ks[5], (N_A_LAYERS, DEC_BATCH, CONV_WIDTH - 1, D_MODEL), 1.0),
        "page_table": jax.random.permutation(ks[6], n_pool)[:n_used].reshape(DEC_BATCH, n_pages).astype(jnp.int32),
        "meta_tokens": nrm(ks[7], (N_META, D_MODEL), 1.0),
        "norm_mix": 1.0 + nrm(ks[8], (DEPTH, D_MODEL), 0.02),
        "norm_mlp": 1.0 + nrm(ks[9], (DEPTH, D_MODEL), 0.02),
        "conv_w_in": nrm(ks[10], (N_A_LAYERS, D_MODEL, 3 * D_MODEL), D_MODEL ** -0.5),
        "conv_w": nrm(ks[11], (N_A_LAYERS, CONV_WIDTH, D_MODEL), CONV_WIDTH ** -0.5),
        "conv_w_out": nrm(ks[12], (N_A_LAYERS, D_MODEL, D_MODEL), D_MODEL ** -0.5),
        "norm_kv": 1.0 + nrm(ks[13], (D_MODEL,), 0.02),
        "w_kv": nrm(ks[14], (D_MODEL, 2 * ATTN_DIM), D_MODEL ** -0.5),
        "k_norm": 1.0 + nrm(ks[15], (HEAD_DIM,), 0.02),
        "w_f": nrm(ks[16], (D_MODEL, N_HEADS), 0.5 * D_MODEL ** -0.5),
        "b_f": FORGET_BIAS + nrm(ks[17], (N_HEADS,), 0.1),
        "w_q": nrm(ks[18], (N_B_LAYERS, D_MODEL, ATTN_DIM), D_MODEL ** -0.5),
        "q_norm": 1.0 + nrm(ks[19], (N_B_LAYERS, HEAD_DIM), 0.02),
        "w_o": nrm(ks[20], (N_B_LAYERS, ATTN_DIM, D_MODEL), ATTN_DIM ** -0.5),
        "mlp_w1": nrm(ks[21], (DEPTH, D_MODEL, D_FF), D_MODEL ** -0.5),
        "mlp_w2": nrm(ks[22], (DEPTH, D_FF, D_MODEL), D_FF ** -0.5),
    }

def reference(x_prompt, x_sample, cache_k, cache_v, cache_logf, state_conv, page_table, meta_tokens,
              norm_mix, norm_mlp, conv_w_in, conv_w, conv_w_out, norm_kv, w_kv, k_norm, w_f, b_f,
              w_q, q_norm, w_o, mlp_w1, mlp_w2):
    weights = (norm_mix, norm_mlp, conv_w_in, conv_w, conv_w_out, norm_kv, w_kv, k_norm, w_f, b_f,
               w_q, q_norm, w_o, mlp_w1, mlp_w2)

    nb = x_prompt.shape[0]
    meta = jnp.broadcast_to(meta_tokens[None].astype(x_prompt.dtype), (nb, N_META, D_MODEL))
    xp = jnp.concatenate([meta, x_prompt], axis=1)
    conv0 = jnp.zeros((N_A_LAYERS, nb, CONV_WIDTH - 1, D_MODEL), x_prompt.dtype)
    hp, conv_prompt, k_prompt, v_prompt, logf_prompt = decoder_trunk(
        xp, conv0, prompt_prepare, prompt_attend, *weights)
    y_prompt = hp[:, N_META:]

    past_k = gather_pages(cache_k, page_table)
    past_v = gather_pages(cache_v, page_table)
    past_logf = gather_pages(cache_logf, page_table)
    prep = functools.partial(sample_prepare, past_k=past_k, past_v=past_v, past_logf=past_logf)
    y_sample, conv_sample, k_sample, v_sample, logf_sample = decoder_trunk(
        x_sample, state_conv, prep, sample_attend, *weights)

    return (y_prompt, y_sample, k_prompt, v_prompt, logf_prompt, conv_prompt,
            k_sample, v_sample, logf_sample, conv_sample)


_drawn_inputs = setup_inputs


def setup_inputs(seed=0):
    import zlib

    import numpy as np

    out = dict(_drawn_inputs(seed))
    spreads = {}
    factors = {'norm_mlp': 2.736, 'norm_kv': 2.733, 'k_norm': 8.193, 'q_norm': 8.0, 'cache_logf': 16.632}
    for name, (base, spread) in spreads.items():
        noise = np.random.default_rng([zlib.crc32(name.encode()), seed]).standard_normal(out[name].shape)
        drawn = base * np.exp(spread * noise) if base else spread * noise
        out[name] = __import__('jax').numpy.asarray(drawn.astype(out[name].dtype))
    for name, factor in factors.items():
        out[name] = (out[name] * factor).astype(out[name].dtype)
    return out
```

```python
from contextlib import ExitStack

import numpy as np

import concourse.bass as bass
from concourse import mybir

F32 = mybir.dt.float32
F32R = mybir.dt.float32r
I32 = mybir.dt.int32
ALU = mybir.AluOpType
ACT = mybir.ActivationFunctionType

P = 128
D = 1024
KC = D // P
SEQ = 1024
META = 16
NPR = SEQ + META
DB, DQ = 8, 4
NS = DB * DQ
TOK = NPR + NS
G = 3
GW = 358
T = G * GW
NH, HD = 16, 64
PAST, PAGE = 256, 128
NPAGE = PAST // PAGE
CW = 3
NT = 9
LAST = TOK - 128 * (NT - 1)
LASTP = NPR - 128 * (NT - 1)
FF_BLK = 4
EPS = 1e-6
SCALE = HD ** -0.5
MASKED = -1e30 / SCALE

U_IN = 0
U_OUT = U_IN + 3 * KC
U_MLP = [U_OUT + KC, 0]
U_K = U_MLP[0] + 2 * KC * FF_BLK
U_V = U_K + KC
U_Q = U_V + KC
U_O = U_Q + KC
U_MLP[1] = U_O + KC
N_UNITS = U_MLP[1] + 2 * KC * FF_BLK

G_MIX = [0, KC]
G_MLP = [2 * KC, 3 * KC]
G_KV = 4 * KC
G_CONV = 5 * KC
G_KN = G_CONV + CW * KC
G_QN = G_KN + 1
N_VEC = G_QN + 1

SPLITS = [G_MIX[0], G_MLP[0], G_KV, G_MIX[1], G_MLP[1]]

AX_IN = 0
AX_VEC = AX_IN + 2 * NT
AX_ST = [0, 0, 0, 0]
AX_ST[0] = AX_VEC + 2
AX_CONV = AX_ST[0] + G
AX_ST[1] = AX_CONV + 2
AX_ST[2] = AX_ST[1] + G
AX_F = AX_ST[2] + G
AX_K = AX_F + G
AX_V = AX_K + 6 * KC
AX_LF = AX_V + 3 * KC
AX_Q = AX_LF + 1
AX_ST[3] = AX_Q + 3 * KC
AX_Y = AX_ST[3] + G

STEPS = 2 * NT
BLOCKS = [min(t + 1, NT) for t in range(NT)]
GROUPS = [[range(4 * g, min(4 * g + 4, b)) for g in range(-(-b // 4))] if t < NT - 1 else [range(b)]
          for t, b in enumerate(BLOCKS)]
TURNS = [range(0, 3), range(3, 5), range(5, 7), range(7, 9)]
RING_P, RING_S, RING_O = {}, {}, []
RING = 0
for _n in range(STEPS):
    if (_n + 2) % NT == NT - 1:
        RING_S[_n + 2] = RING
        RING += 1
    RING_P[_n] = RING
    RING += len(GROUPS[_n % NT])
    if _n == 1:
        RING_O = RING
        RING += len(TURNS)
N_GROUPS = 2 * sum(len(g) for g in GROUPS)
KEYS = PAST + NS


def trunk(nc, a, out):
    ctx = ExitStack()
    with ctx:
        at = [nc.sbuf_base + (-nc.sbuf_base) % 32]

        def place(name, shape, dt=F32, offset=None):
            size = 4 * int(np.prod(shape[1:]))
            size += -size % 32
            if offset is None:
                offset = at[0]
                at[0] += size
            return nc.alloc_sbuf_tensor_at(name, shape, dt, offset=offset), offset + size

        ACC, _ = place("acc", [P, KC, T])
        hid0 = at[0]
        HH, hid1 = place("hid_hi", [P, KC, T], F32R)
        HL, _ = place("hid_lo", [P, KC, T], F32R)
        KS, _ = place("k_all", [P, KC, T], offset=hid0)
        QS, _ = place("q_all", [P, KC, T], offset=hid1)
        IN, _ = place("tokens_in", [P, NT, D], offset=hid0)
        RAW, _ = place("w_raw", [P, 2, KC, P])
        WH, _ = place("w_hi", [P, 2, KC, P], F32R)
        WL, _ = place("w_lo", [P, 2, KC, P], F32R)
        ident, _ = place("ident", [P, P])
        ones, _ = place("ones", [P, P], F32R)
        heads1, _ = place("ones_per_head", [P, P], F32R)
        vecs, _ = place("vectors", [P, N_VEC])
        epst, _ = place("eps", [P, 1])
        lf0 = at[0]
        LF, _ = place("gate_logits", [NH, T])
        CST, cst1 = place("conv_states", [P, KC, DB * (CW - 1)], offset=lf0)
        UL, _ = place("conv_last", [P, KC, (DB + 1) * (CW - 1)], offset=cst1)
        VIN, _ = place("vectors_in", [N_VEC, P], offset=lf0 + 1088)
        att0 = at[0]
        XH, _ = place("x_hi", [P, KC, T], F32R)
        XL, _ = place("x_lo", [P, KC, T], F32R)
        R, _ = place("rms_inv", [P, T])
        t10 = at[0]
        T1, t1e = place("t1", [P, T])
        t20 = at[0]
        T2, _ = place("t2", [P, T + 16])
        T1R, _ = place("t1_r", [P, T], F32R, offset=t10)
        T2R, _ = place("t2_r", [P, T], F32R, offset=t20)
        kw0 = at[0]
        KW, kwe = place("k_work", [P, 2, T])
        OT, _ = place("out_tiles", [P, NT, P])
        att1 = at[0]
        assert att1 <= nc.sbuf_usable_end - 24, att1
        STI, _ = place("states_in", [DB * (CW - 1), D], offset=kw0)
        CO, _ = place("conv_out", [(DB + 1) * (CW - 1), D], offset=kw0)
        YO, _ = place("y_out", [P, 4, D], offset=att0)
        WFR, o = place("wf_raw", [P, KC, NH], offset=kwe)
        WFH, o = place("wf_hi", [P, KC, NH], F32R, offset=o)
        WFL, o = place("wf_lo", [P, KC, NH], F32R, offset=o)
        BF, _ = place("b_f", [NH, 1], offset=att1)
        assert att1 + 32 <= nc.sbuf_usable_end
        slot = 4 * T + (-4 * T) % 32
        Z, ZN, ZE, ZU = (place(n, [NH, T], offset=hid1 + slot * m)[0]
                         for m, n in enumerate(("gate_z", "gate_neg", "gate_exp", "gate_exp1")))
        LT, _ = place("logf_tiles", [P, NT, NH], offset=hid1 + slot * 5)
        C8, _ = place("minus_8_sums", [NH, NPR], offset=hid1 + slot * 6)
        c_rows = nc.dram_tensor("c_rows", [NH, NPR], F32, kind="Internal").ap()

        def areas(start):
            where = [start]

            def put(name, shape, dt=F32):
                t, where[0] = place(name, shape, dt, offset=where[0])
                assert where[0] <= att1, (name, where[0] - att1)
                return t
            return put, where

        put, prompt_end = areas(att0)
        QP = put("q_split", [P, 2, NPR], F32R)
        KP = put("k_twice", [P, 2, NPR], F32R)
        KL = put("k_lo", [P, NPR], F32R)
        NEGC = put("minus_8_c", [P, 2, NPR])
        VRAW = put("v_raw", [P, NT, P])
        VV = put("v_split", [P, 2, NT, 2, HD], F32R)
        PR = put("probs", [P, 3, NPR])
        PTH = put("probs_t_hi", [P, 2, SEQ], F32R)
        PTL = put("probs_t_lo", [P, 2, SEQ], F32R)
        OS = put("o_tiles", [P, NT, 2, HD])
        OP = put("o_part", [P, 2, HD])
        MASKF = put("mask_f32", [P, P])
        MASK = put("mask", [P, P], F32R)
        IDR = put("ident_r", [P, P], F32R)
        NEGM, RSUM, RINV = (put(n, [P, 8]) for n in ("minus_max", "row_sum", "row_inv"))
        put, _ = areas(prompt_end[0])
        KPG = put("k_page", [P, 2, NPAGE, D])
        put, decode_end = areas(att0)
        VPG = put("v_page", [P, NPAGE, D])
        VPH = put("v_page_hi", [P, NPAGE, D], F32R)
        VPL = put("v_page_lo", [P, NPAGE, D], F32R)
        VDH = put("v_new_hi", [NS, D], F32R)
        VDL = put("v_new_lo", [NS, D], F32R)
        KTH = put("k_t_hi", [P, KC, KEYS], F32R)
        KTL = put("k_t_lo", [P, KC, KEYS], F32R)
        QBW = (NH * DQ + 2 * DQ) * KC + 2 * DQ
        QBH = put("q_blocks_hi", [P, QBW], F32R)
        QBL = put("q_blocks_lo", [P, QBW], F32R)
        CSF = put("past_sums", [NH, PAST + DB * (KEYS + DQ)])
        CSH = put("sums_hi", [NH, KEYS], F32R)
        CSL = put("sums_lo", [NH, KEYS], F32R)
        LPG = put("logf_page", [P, DB * NPAGE, NH])
        HQ = NH * DQ
        EXF = put("expand_f32", [NH, HQ])
        EX = put("expand", [NH, HQ], F32R)
        MW = put("mask_wide", [HQ, NH, DQ])
        M4 = put("mask_new", [HQ, DQ])
        MB = put("mask_by_seq", [HQ, DB, NS])
        MBC = put("mask_row", [HQ, 2, KEYS])
        SD = put("d_probs", [HQ, 2, KEYS])
        DPH = put("d_probs_t_hi", [P, NPAGE + 1, HQ], F32R)
        DPL = put("d_probs_t_lo", [P, NPAGE + 1, HQ], F32R)
        DST = put("d_stats", [HQ, 3, 2])
        PTAB = put("page_ids", [1, DB * NPAGE], I32)
        assert decode_end[0] <= prompt_end[0]
        CS = CSF[:, 0:DB * KEYS].rearrange("h (b k) -> h b k", b=DB)
        CS_NEW = CSF[:, PAST:PAST + DB * (KEYS + DQ)].rearrange("h (b k) -> h b k", b=DB)[:, :, 0:DQ]
        UP = T2[:, 0:CW - 1 + NPR]
        US = T2[:, CW - 1 + NPR:CW - 1 + NPR + DB * (DQ + CW - 1)].rearrange("p (b t) -> p b t", b=DB)
        PS = ctx.enter_context(nc.psum_tensor("ps", [P, 8, 512], F32))

        def banks(x):
            return x.rearrange("p (g w) -> p g w", g=G)

        def sem(name):
            return ctx.enter_context(nc.semaphore(name))

        in_loaded = [sem(f"in_loaded{t}") for t in range(NT)]
        vec_loaded, state_loaded, gate_w_loaded = sem("vec_loaded"), sem("state_loaded"), sem("gate_w_loaded")
        w_loaded = [sem("w_loaded0"), sem("w_loaded1")]
        w_hi, w_lo = sem("w_hi"), sem("w_lo")
        unit_done, unit_read = sem("unit_done"), sem("unit_read")
        aux_done, aux_read = sem("aux_done"), sem("aux_read")
        const_ready, zero_ready, heads_zero = sem("const_ready"), sem("zero_ready"), sem("heads_zero")
        x_hi, x_lo, x_sq, x_ssq = sem("x_hi"), sem("x_lo"), sem("x_sq"), sem("x_ssq")
        ssq_hi, ssq_lo, rms_ready = sem("ssq_hi"), sem("ssq_lo"), sem("rms_ready")
        h_raw, hid_hi, hid_lo = sem("h_raw"), sem("hid_hi"), sem("hid_lo")
        u_ready, u_last, conv_step = sem("u_ready"), sem("u_last"), sem("conv_step")
        conv_stored = sem("conv_stored")
        z_sq, z_hi, z_lo, z_inv, z_fin = sem("z_sq"), sem("z_hi"), sem("z_lo"), sem("z_inv"), sem("z_fin")
        k_kept, kv_stored = sem("k_kept"), sem("kv_stored")
        gate_hi, gate_lo = sem("gate_hi"), sem("gate_lo")
        bf_loaded, gate_step, gate_act = sem("bf_loaded"), sem("gate_step"), sem("gate_act")
        logf_stored, c_stored = sem("logf_stored"), sem("c_stored")
        lt_kept = sem("lt_kept")
        p_const, p_round, v_zero = sem("p_const"), sem("p_round"), sem("v_zero")
        q_hi, q_lo, k_hi, k_dup, k_lo = sem("q_hi"), sem("q_lo"), sem("k_hi"), sem("k_dup"), sem("k_lo")
        v_loaded, v_hi, v_lo = sem("v_loaded"), sem("v_hi"), sem("v_lo")
        c_loaded = [sem("c_loaded0"), sem("c_loaded1")]
        s_done, s_used, e_done = sem("s_done"), sem("s_used"), sem("e_done")
        ring_done, ring_free, pt_hi = sem("ring_done"), sem("ring_free"), sem("pt_hi")
        pv_done, inv_ready, o_part, o_out = sem("pv_done"), sem("inv_ready"), sem("o_part"), sem("o_out")
        ids_loaded, lp_loaded, vn_loaded = sem("ids_loaded"), sem("lp_loaded"), sem("vn_loaded")
        dk_loaded, dv_loaded = [sem("dk_loaded0"), sem("dk_loaded1")], sem("dv_loaded")
        d_const, d_mask, d_sums, new_hi, new_lo = (sem("d_const"), sem("d_mask"), sem("d_sums"),
                                                   sem("new_hi"), sem("new_lo"))
        past_done, past_kept, mb_ready = sem("past_done"), sem("past_kept"), sem("mb_ready")
        dt_done, dt_hi, dt_used = sem("dt_done"), sem("dt_hi"), sem("dt_used")
        qc_hi, qc_lo, dv_hi, dv_lo = sem("qc_hi"), sem("qc_lo"), sem("dv_hi"), sem("dv_lo")
        ds_done, ds_used, de_done, dn_done = sem("ds_done"), sem("ds_used"), sem("de_done"), sem("dn_done")
        dp_done, dp_hi, dp_used = sem("dp_done"), sem("dp_hi"), sem("dp_used")
        do_done, do_used = sem("do_done"), sem("do_used")
        o_hi, o_lo = sem("o_hi"), sem("o_lo")
        y_stored = [sem(f"y_stored{i}") for i in range(4)]

        def ge(eng, s, value):
            if not isinstance(value, (int, np.integer)) or value > 0:
                eng.wait_ge(s, value)

        wait_value = {}

        def ge_apart(eng, s, value):
            if not isinstance(value, (int, np.integer)):
                if eng not in wait_value:
                    wait_value[eng] = eng.alloc_register("wait_value")
                eng.reg_add(wait_value[eng], value, 0)
                eng.wait_ge(const_ready, 1)
                eng.wait_ge(s, wait_value[eng])
            else:
                ge(eng, s, value)

        def sides(t):
            return 128 * t, min(128, TOK - 128 * t)

        pe, act, dve, pool, sp = nc.tensor, nc.scalar, nc.vector, nc.gpsimd, nc.sync

        def load_unit(w, row0, col0, c, i=0, stride=2):
            u = c + stride * i
            ge_apart(sp, w_lo, u - 1)
            src = w.rearrange("(k p) n -> p k n", p=P)[:, row0:row0 + KC, bass.ds(col0, P)] \
                if isinstance(row0, int) else \
                w.rearrange("(k p) n -> p k n", p=P)[:, bass.ds(row0, KC), bass.ds(col0, P)]
            sp.dma_start(RAW[:, c % 2], src).then_inc(w_loaded[c % 2], 16)

        def round_unit(c, i=0, stride=2):
            if isinstance(i, int) and c + stride * i >= N_UNITS:
                return
            u, s = c + stride * i, c % 2
            act.wait_ge(w_loaded[s], 16 * (c // 2 + 1) + (16 * stride // 2) * i)
            ge(act, unit_done, u - 1)
            act.activation(WH[:, s], RAW[:, s], ACT.Copy).then_inc(w_hi, 1)

        def cut_unit(c, i=0, stride=2):
            if isinstance(i, int) and c + stride * i >= N_UNITS:
                return
            u, s = c + stride * i, c % 2
            dve.wait_ge(w_hi, u + 1)
            dve.tensor_tensor(WL[:, s], RAW[:, s], WH[:, s].bitcast(F32), ALU.subtract).then_inc(w_lo, 1)

        def unit(c, i=0, stride=2, hi=XH, lo=XL, ready=None, mid=None):
            u, s = c + stride * i, c % 2
            pe.wait_ge(w_lo, u + 1)
            ge(pe, unit_read, u - 1)
            for k in range(KC):
                if mid and k in mid:
                    mid[k]()
                if ready:
                    ready(k)
                for n, (w, x) in enumerate(((WH, hi), (WH, lo), (WL, hi))):
                    for g in range(G):
                        mm = pe.matmul(PS[:, G * s + g, 0:GW], w[:, s, k], x[:, k, g * GW:(g + 1) * GW],
                                       start=(k == 0 and n == 0), stop=(k == KC - 1 and n == 2))
            mm.then_inc(unit_done, 1)

        def result(c):
            return PS[:, G * (c % 2):G * (c % 2) + G, 0:GW]

        def residual_hi(split, m, square=None):
            act.activation(XH[:, m], ACC[:, m], ACT.Copy,
                           scale=vecs[:, bass.ds(SPLITS[split] + m, 1)]).then_inc(x_hi, 1)
            if square is not None:
                ge_apart(act, x_ssq, 8 * square + m)
                act.activation(T1[:, :], ACC[:, m], ACT.Square).then_inc(x_sq, 1)

        def residual_lo(split, m):
            dve.wait_ge(x_hi, 8 * split + m + 1)
            dve.scalar_tensor_tensor(XL[:, m], ACC[:, m], vecs[:, bass.ds(SPLITS[split] + m, 1)],
                                     XH[:, m].bitcast(F32), ALU.mult, ALU.subtract).then_inc(x_lo, 1)

        def residual_sum(f, m):
            pool.wait_ge(x_sq, 8 * f + m + 1)
            if isinstance(m, int) and m == 0:
                pool.tensor_copy(T2[:, 0:T], T1[:, :]).then_inc(x_ssq, 1)
            else:
                pool.wait_ge(x_ssq, 8 * f + m)
                pool.tensor_tensor(T2[:, 0:T], T2[:, 0:T], T1[:, :], ALU.add).then_inc(x_ssq, 1)

        def rms_split_hi(s):
            act.wait_ge(x_ssq, 8 * (s + 1))
            act.activation(T1R[:, :], T2[:, 0:T], ACT.Copy).then_inc(ssq_hi, 1)

        def rms_split_lo(s):
            dve.wait_ge(ssq_hi, s + 1)
            dve.tensor_tensor(T2R[:, :], T2[:, 0:T], T1R[:, :].bitcast(F32), ALU.subtract).then_inc(ssq_lo, 1)

        def column_sums(first, weights, wait):
            wait()
            for g in range(G):
                b = 6 + (first + g) % 2 if isinstance(first, int) else 6 + (first[0] + g) % 2
                n = first if isinstance(first, int) else first[1]
                ge(pe, aux_read, n + g - 1)
                for x, stop in ((T1R, False), (T2R, True)):
                    mm = pe.matmul(PS[:, b, 0:GW], weights[:, :], x[:, g * GW:(g + 1) * GW],
                                   start=not stop, stop=stop)
                mm.then_inc(aux_done, 1)

        def rms_root(s):
            for g in range(G):
                n = AX_ST[s] + g
                act.wait_ge(aux_done, n + 1)
                act.activation(R[:, g * GW:(g + 1) * GW], PS[:, 6 + n % 2, 0:GW], ACT.Sqrt,
                               scale=1.0 / D, bias=epst[:, 0:1]).then_inc(aux_read, 1)

        def rms_inverse(s):
            dve.wait_ge(aux_read, AX_ST[s] + G)
            dve.reciprocal(R[:, :], R[:, :]).then_inc(rms_ready, 1)
            dve.wait_ge(rms_ready, s + 1)

        def rms_sums(s):
            column_sums(AX_ST[s], ones, lambda: pe.wait_ge(ssq_lo, s + 1))

        def x_ready(split):
            return lambda k: pe.wait_ge(x_lo, 8 * split + k + 1)

        def turn_tokens(par, n):
            for g in range(G):
                pe_bank = 6 + (n[0] + g) % 2
                ge_apart(pe, aux_read, n[1] + g - 1)
                for t in range(4 * g, min(4 * g + 4, NT)):
                    tok, rows = sides(t)
                    mm = pe.transpose(PS[0:rows, pe_bank, P * (t % 4):P * (t % 4) + P],
                                      KW[:, par, tok:tok + rows], ident[:, :])
                mm.then_inc(aux_done, 1)

        def keep_tokens(n, stored):
            ge(act, kv_stored, 48 * stored)
            for g in range(G):
                act.wait_ge(aux_done, n[1] + g + 1)
                b = 6 + (n[0] + g) % 2
                if g < 2:
                    act.activation(OT[:, 4 * g:4 * g + 4, :].rearrange("p t c -> p (t c)"), PS[:, b, :],
                                   ACT.Copy).then_inc(aux_read, 1)
                else:
                    act.activation(OT[0:LAST, NT - 1, :], PS[0:LAST, b, 0:P], ACT.Copy).then_inc(aux_read, 1)

        def store_tokens(n, prompt, decode, m):
            act.wait_ge(aux_read, n[1] + G)
            full = P * (NT - 1)
            rows = prompt[0].rearrange("t h d -> t (h d)")
            act.dma_start(rows[0:full, bass.ds(P * m, P)].rearrange("(t p) c -> p t c", p=P),
                          OT[:, 0:NT - 1, :]).then_inc(kv_stored, 16)
            act.dma_start(rows[full:NPR, bass.ds(P * m, P)], OT[0:LASTP, NT - 1, :]).then_inc(kv_stored, 16)
            act.dma_start(decode.rearrange("b t h d -> (b t) (h d)")[:, bass.ds(P * m, P)],
                          OT[LASTP:LAST, NT - 1, :]).then_inc(kv_stored, 16)

        def ax(first, stride, i):
            return (first, first + stride * i)


        def halves(hh):
            return slice(HD * hh, HD * hh + HD), slice(HD - HD * hh, P - HD * hh)

        def step(n):
            hh, i = n // NT, n % NT
            return hh, i, (P if i < NT - 1 else LASTP)

        def ring(m, idx):
            if isinstance(m, int) and m == 0:
                return idx if idx < RING_O else idx - len(TURNS)
            return RING * m + idx - len(TURNS)

        def pt_index(m, n, g):
            return N_GROUPS * m + sum(len(GROUPS[x % NT]) for x in range(n)) + g

        def prep_act(m, hh, part):
            own, _ = halves(hh)
            if part == 0:
                ge_apart(act, s_done, STEPS * m + NT * hh - NT)
                act.activation(QP[own, hh], QS[own, m, 0:NPR], ACT.Copy).then_inc(q_hi, 1)
                act.activation(KP[own, hh], KS[own, m, 0:NPR], ACT.Copy).then_inc(k_hi, 1)
            else:
                if hh == 0:
                    act.wait_ge(v_loaded, 32 * (m + 1))
                ge(act, pv_done, STEPS * m + NT * hh - NT)
                act.activation(VV[:, hh, :, 0], VRAW[:, :, HD * hh:HD * hh + HD], ACT.Copy)\
                   .then_inc(v_hi, 1)

        def prep_dve(m, hh):
            own, other = halves(hh)
            dve.wait_ge(q_hi, 2 * m + hh + 1)
            dve.tensor_tensor(QP[other, hh], QS[own, m, 0:NPR], QP[own, hh].bitcast(F32), ALU.subtract)\
               .then_inc(q_lo, 1)
            dve.wait_ge(k_hi, 2 * m + hh + 1)
            dve.tensor_copy(KP[other, hh], KP[own, hh]).then_inc(k_dup, 1)

        def prep_pool(m, hh):
            own, _ = halves(hh)
            ge(pool, v_lo, 2 * m + hh)
            ge_apart(pool, k_hi, 2 * m + hh + 1)
            pool.tensor_tensor(KL[own, :], KS[own, m, 0:NPR], KP[own, hh].bitcast(F32), ALU.subtract)\
                .then_inc(k_lo, 1)
            pool.wait_ge(k_lo, 2 * m + hh + 1)
            pool.wait_ge(v_hi, 2 * m + hh + 1)
            pool.tensor_tensor(VV[:, hh, :, 1], VRAW[:, :, HD * hh:HD * hh + HD],
                               VV[:, hh, :, 0].bitcast(F32), ALU.subtract).then_inc(v_lo, 1)

        def logits(m, n):
            hh, i, rows = step(n % STEPS)
            if n >= STEPS:
                m, n = m + 1, n - STEPS
            s, b0 = STEPS * m + n, 2 * (n % 2)
            own, _ = halves(hh)
            if i == 0:
                for ready in (q_lo, k_dup, k_lo):
                    pe.wait_ge(ready, 2 * m + hh + 1)
            ge(pe, s_used, s - 1)
            q = slice(P * i, P * i + rows)

            def part(out, cols, diagonal):
                mm = pe.matmul(out, QP[:, hh, q], KP[:, hh, cols], start=True, stop=False)
                mm = pe.matmul(out, QP[own, hh, q], KL[own, cols], start=False, stop=not diagonal)
                return mm

            wide = min(P * (i + 1), SEQ)
            for c0 in range(0, wide, 512):
                w = min(512, wide - c0)
                diagonal = i < NT - 1 and c0 + w == wide
                mm = part(PS[0:rows, b0 + c0 // 512, 0:w], slice(c0, c0 + w), diagonal)
                if diagonal:
                    mm = pe.matmul(PS[:, b0 + c0 // 512, w - P:w], IDR[:, :], MASK[:, :], start=False, stop=True)
            mm.then_inc(s_done, 1)
            if i == NT - 1:
                use, bank = ring(m, RING_S[n]), 4 + RING_S[n] % 2
                pe.wait_ge(ring_free, use - 1)
                out = PS[0:rows, bank, 0:LASTP]
                part(out, slice(SEQ, NPR), True)
                pe.matmul(out, IDR[0:rows, 0:rows], MASK[0:rows, 0:LASTP], start=False, stop=True)\
                  .then_inc(ring_done, 1)

        def max_logits(m, n):
            hh, i, rows = step(n % STEPS)
            if n >= STEPS:
                m, n = m + 1, n - STEPS
            s, b0, k = STEPS * m + n, 2 * (n % 2), n % 6
            if i == 0:
                dve.wait_ge(c_loaded[hh], 16 * (m + 1))
            wide = min(P * (i + 1), SEQ)
            first = 3e38
            if i == NT - 1:
                use, bank = ring(m, RING_S[n]), 4 + RING_S[n] % 2
                ge_apart(dve, ring_done, use + 1)
                first = NEGM[0:rows, 6 + hh:7 + hh]
                dve.tensor_tensor_reduce(out=PR[0:rows, n % 3, SEQ:NPR], in0=PS[0:rows, bank, 0:LASTP],
                                         in1=NEGC[0:rows, hh, SEQ:NPR], scale=-SCALE, scalar=3e38,
                                         op0=ALU.add, op1=ALU.min, accum_out=first).then_inc(ring_free, 1)
                dve.wait_ge(ring_free, use + 1)
            ge_apart(dve, s_done, s + 1)
            dve.tensor_tensor_reduce(out=PR[0:rows, n % 3, 0:wide],
                                     in0=PS[0:rows, b0:b0 + 2, :].rearrange("p b w -> p (b w)")[:, 0:wide],
                                     in1=NEGC[0:rows, hh, 0:wide], scale=-SCALE, scalar=first,
                                     op0=ALU.add, op1=ALU.min, accum_out=NEGM[0:rows, k:k + 1])\
               .then_inc(s_used, 1)

        def exp_logits(m, n):
            hh, i, rows = step(n % STEPS)
            if n >= STEPS:
                m, n = m + 1, n - STEPS
            k, wide = n % 6, (P * (i + 1) if i < NT - 1 else NPR)
            act.wait_ge(s_used, STEPS * m + n + 1)
            x = PR[0:rows, n % 3, 0:wide]
            act.activation(x, x, ACT.Exp, scale=-1.0, bias=NEGM[0:rows, k:k + 1],
                           accum_out=RSUM[0:rows, k:k + 1]).then_inc(e_done, 1)

        def pt_groups(n):
            i = n % NT
            w = P if i < NT - 1 else LASTP
            return [(RING_P[n] + g, g, blocks, w) for g, blocks in enumerate(GROUPS[i])]

        def turn_probs(m, n):
            hh, i, rows = step(n)
            ge_apart(pe, e_done, STEPS * m + n + 1)
            for idx, g, blocks, w in pt_groups(n):
                ge_apart(pe, ring_free, ring(m, idx) - 1)
                for x, j in enumerate(blocks):
                    keys = min(P, NPR - P * j)
                    mm = pe.transpose(PS[0:keys, 4 + idx % 2, w * x:w * x + rows],
                                      PR[0:rows, n % 3, P * j:P * j + keys], ident[0:rows, 0:rows])
                mm.then_inc(ring_done, 1)

        def probs_hi(m, n):
            ge(act, pv_done, STEPS * m + n - 1)
            for idx, g, blocks, w in pt_groups(n):
                act.wait_ge(ring_done, ring(m, idx) + 1)
                a0, a1 = w * blocks[0], w * (blocks[-1] + 1)
                act.activation(PTH[:, n % 2, a0:a1], PS[:, 4 + idx % 2, 0:a1 - a0], ACT.Copy)\
                   .then_inc(pt_hi, 1)

        def probs_lo(m, n):
            for idx, g, blocks, w in pt_groups(n):
                dve.wait_ge(pt_hi, pt_index(m, n, g) + 1)
                a0, a1 = w * blocks[0], w * (blocks[-1] + 1)
                dve.tensor_tensor(PTL[:, n % 2, a0:a1], PS[:, 4 + idx % 2, 0:a1 - a0],
                                  PTH[:, n % 2, a0:a1].bitcast(F32), ALU.subtract).then_inc(ring_free, 1)

        def inverse_sums(m, n):
            rows, k = step(n)[2], n % 6
            dve.wait_ge(e_done, STEPS * m + n + 1)
            dve.reciprocal(RINV[0:rows, k:k + 1], RSUM[0:rows, k:k + 1]).then_inc(inv_ready, 1)

        def weigh_values(m, n):
            hh, i, rows = step(n)
            s, w = STEPS * m + n, (P if i < NT - 1 else LASTP)
            idx = pt_groups(n)[-1][0]
            if i == 0:
                pe.wait_ge(v_lo, 2 * m + hh + 1)
            pe.wait_ge(ring_free, ring(m, idx) + 1)
            ge(pe, o_out, s - 1)
            last = BLOCKS[i] - 1
            for j in range(BLOCKS[i]):
                keys = min(P, NPR - P * j)
                pe.matmul(PS[0:rows, 6 + n % 2, 0:P], PTH[0:keys, n % 2, w * j:w * j + rows],
                          VV[0:keys, hh, j].rearrange("p x d -> p (x d)"), start=(j == 0), stop=False)
                mm = pe.matmul(PS[0:rows, 6 + n % 2, 0:HD], PTL[0:keys, n % 2, w * j:w * j + rows],
                               VV[0:keys, hh, j, 0], start=False, stop=(j == last))
            mm.then_inc(pv_done, 1)

        def output_part(m, n):
            rows, k, s = step(n)[2], n % 6, STEPS * m + n
            act.wait_ge(inv_ready, s + 1)
            act.wait_ge(pv_done, s + 1)
            ge(act, o_out, s - 1)
            act.activation(OP[0:rows, n % 2], PS[0:rows, 6 + n % 2, HD:P], ACT.Copy,
                           scale=RINV[0:rows, k:k + 1]).then_inc(o_part, 1)

        def output_tile(m, n):
            hh, i, rows = step(n)
            k = n % 6
            dve.wait_ge(o_part, STEPS * m + n + 1)
            dve.scalar_tensor_tensor(OS[0:rows, i, hh], PS[0:rows, 6 + n % 2, 0:HD], RINV[0:rows, k:k + 1],
                                     OP[0:rows, n % 2], ALU.mult, ALU.add).then_inc(o_out, 1)

        def turn_output(m):
            pe.wait_ge(o_out, STEPS * m)
            for g, tiles in enumerate(TURNS):
                idx = RING_O + g
                pe.wait_ge(ring_free, RING * m + idx - len(TURNS) - 1 - (RING_O if isinstance(m, int) and m == KC else 0))
                for x, t in enumerate(tiles):
                    rows = min(P, NPR - P * t)
                    mm = pe.transpose(PS[:, 4 + idx % 2, P * x:P * x + rows],
                                      OS[0:rows, t].rearrange("p h d -> p (h d)"), ident[0:rows, 0:rows])
                mm.then_inc(ring_done, 1)

        def keep_output(m):
            for g, tiles in enumerate(TURNS):
                idx = RING_O + g
                dve.wait_ge(ring_done, RING * m + idx - len(TURNS) + 1
                            - (RING_O if isinstance(m, int) and m == KC else 0))
                t0, t1 = P * tiles[0], min(P * (tiles[-1] + 1), NPR)
                dve.tensor_copy(QS[:, m - 1, t0:t1], PS[:, 4 + idx % 2, 0:t1 - t0]).then_inc(ring_free, 1)

        PROMPT_GROUPS = RING * KC

        def d_turn_keys(i, c):
            b = c + 2 * i
            pe.wait_ge(dk_loaded[c], 32 * (i + 1))
            for g in range(NPAGE):
                for h in range(2):
                    x = 2 * g + h
                    ge(pe, dt_used, 4 * b + x - 1)
                    for k in range(4):
                        f = P * (4 * h + k)
                        mm = pe.transpose(PS[:, x % 2, P * k:P * k + P], KPG[:, c, g, f:f + P], ident[:, :])
                    mm.then_inc(dt_done, 1)

        def d_groups():
            return [(2 * g + h, (slice(None), slice(4 * h, 4 * h + 4), slice(PAGE * g, PAGE * g + PAGE)))
                    for g in range(NPAGE) for h in range(2)]

        def ps_turned(x):
            return PS[:, x % 2, :].rearrange("p (k t) -> p k t", k=4)

        def q_blocks(t, hh):
            w = NH * DQ + 2 * DQ
            return t[HD * hh:HD * hh + HD, DQ * hh:DQ * hh + w * KC].rearrange("p (m x) -> p m x", x=w)[:, :, 0:DQ]

        def d_hi(i, c):
            b = c + 2 * i
            ge(act, ds_done, b)
            for x, to in d_groups():
                act.wait_ge(dt_done, 4 * b + x + 1)
                act.activation(KTH[to], ps_turned(x), ACT.Copy).then_inc(dt_hi, 1)
            for hh in range(2):
                act.activation(q_blocks(QBH, hh), QS[HD * hh:HD * hh + HD, :, bass.ds(NPR + DQ * b, DQ)],
                               ACT.Copy).then_inc(qc_hi, 1)
            act.activation(CSH[:, :], CS[:, b], ACT.Copy, scale=-1.0 / SCALE).then_inc(qc_hi, 1)

        def d_lo(i, c):
            b = c + 2 * i
            for x, to in d_groups():
                dve.wait_ge(dt_hi, 4 * b + x + 1)
                dve.tensor_tensor(KTL[to], ps_turned(x), KTH[to].bitcast(F32), ALU.subtract).then_inc(dt_used, 1)
            dve.wait_ge(qc_hi, 3 * (b + 1))
            for hh in range(2):
                dve.tensor_tensor(q_blocks(QBL, hh), QS[HD * hh:HD * hh + HD, :, bass.ds(NPR + DQ * b, DQ)],
                                  q_blocks(QBH, hh).bitcast(F32), ALU.subtract).then_inc(qc_lo, 1)
            dve.scalar_tensor_tensor(CSL[:, :], CS[:, b], -1.0 / SCALE, CSH[:, :].bitcast(F32),
                                     ALU.mult, ALU.subtract).then_inc(qc_lo, 1)

        def d_logits(i, c):
            b = c + 2 * i
            pe.wait_ge(dt_used, 4 * (b + 1))
            pe.wait_ge(qc_lo, 3 * (b + 1))
            ge(pe, ds_used, b - 1)
            out = PS[0:HQ, 2 + c, 0:KEYS]
            for m in range(KC):
                for q, k in ((QBH, KTH), (QBH, KTL), (QBL, KTH)):
                    pe.matmul(out, q[:, HQ * m:HQ * m + HQ], k[:, m], start=(m == 0 and q is QBH and k is KTH),
                              stop=False)
            pe.matmul(out, EX[:, :], CSH[:, :], start=False, stop=False)
            pe.matmul(out, EX[:, :], CSL[:, :], start=False, stop=True).then_inc(ds_done, 1)

        def d_max(i, c):
            b = c + 2 * i
            ge_apart(dve, ds_done, b + 1)
            ge_apart(dve, mb_ready, b + 1)
            dve.tensor_tensor_reduce(out=SD[:, c], in0=PS[0:HQ, 2 + c, 0:KEYS], in1=MBC[:, c], scale=-SCALE,
                                     scalar=3e38, op0=ALU.add, op1=ALU.min, accum_out=DST[:, 0, c:c + 1])\
               .then_inc(ds_used, 1)

        def d_exp(i, c):
            act.wait_ge(ds_used, c + 2 * i + 1)
            act.activation(SD[:, c], SD[:, c], ACT.Exp, scale=-1.0, bias=DST[:, 0, c:c + 1],
                           accum_out=DST[:, 1, c:c + 1]).then_inc(de_done, 1)

        def d_norm(i, c):
            b = c + 2 * i
            dve.wait_ge(de_done, b + 1)
            dve.reciprocal(DST[:, 2, c:c + 1], DST[:, 1, c:c + 1]).then_inc(dn_done, 1)
            dve.wait_ge(dn_done, 2 * b + 1)
            dve.tensor_scalar(SD[:, c], SD[:, c], DST[:, 2, c:c + 1], None, ALU.mult).then_inc(dn_done, 1)

        def d_turn_probs(i, c):
            b = c + 2 * i
            ge_apart(pe, dp_used, b - 1)
            ge_apart(pe, dn_done, 2 * b + 2)
            for g in range(NPAGE + 1):
                keys = min(P, KEYS - P * g)
                mm = pe.transpose(PS[0:keys, 4 + c, HQ * g:HQ * g + HQ], SD[:, c, P * g:P * g + keys],
                                  ident[0:HQ, 0:HQ])
            mm.then_inc(dp_done, 1)

        def d_probs_hi(i, c):
            b = c + 2 * i
            act.wait_ge(dp_done, b + 1)
            ge(act, do_done, b)
            act.activation(DPH[:, :, :].rearrange("p g r -> p (g r)"), PS[:, 4 + c, 0:(NPAGE + 1) * HQ],
                           ACT.Copy).then_inc(dp_hi, 1)

        def d_probs_lo(i, c):
            b = c + 2 * i
            dve.wait_ge(dp_hi, b + 1)
            dve.tensor_tensor(DPL[:, :, :].rearrange("p g r -> p (g r)"), PS[:, 4 + c, 0:(NPAGE + 1) * HQ],
                              DPH[:, :, :].rearrange("p g r -> p (g r)").bitcast(F32), ALU.subtract)\
               .then_inc(dp_used, 1)

        def d_values_hi(i, c):
            b = c + 2 * i
            act.wait_ge(dv_loaded, 32 * (b + 1))
            ge(act, do_done, b)
            act.activation(VPH[:, :, :], VPG[:, :, :], ACT.Copy).then_inc(dv_hi, 1)

        def d_values_lo(i, c):
            dve.wait_ge(dv_hi, c + 2 * i + 1)
            dve.tensor_tensor(VPL[:, :, :], VPG[:, :, :], VPH[:, :, :].bitcast(F32), ALU.subtract)\
               .then_inc(dv_lo, 1)

        def d_weigh(i, c):
            b = c + 2 * i
            pe.wait_ge(dv_lo, b + 1)
            pe.wait_ge(dp_used, b + 1)
            ge(pe, do_used, 2 * (b - 1))
            w = 2 * DQ
            for m in range(KC):
                f, r = slice(P * m, P * m + P), slice(w * m, w * m + w)
                for g in range(NPAGE + 1):
                    for n, (vh, vl, pr) in enumerate(((VPH, VDH, DPH), (VPH, VDH, DPL), (VPL, VDL, DPH))):
                        v = vh if n < 2 else vl
                        left = (VPL if n == 2 else VPH)[:, g, f] if g < NPAGE else (VDL if n == 2 else VDH)[:, f]
                        right = pr[:, g, r] if g < NPAGE else pr[0:NS, g, r]
                        mm = pe.matmul(PS[:, 6 + c, r], left, right, start=(g == 0 and n == 0),
                                       stop=(g == NPAGE and n == 2))
            mm.then_inc(do_done, 1)

        def d_output(i, c):
            b = c + 2 * i
            ge_apart(act, do_done, b + 1)
            for hh in range(2):
                half = slice(HD * hh, HD * hh + HD)
                src = PS[half, 6 + c, 0:2 * DQ * KC].rearrange("p (m x) -> p m x", m=KC)
                act.activation(QS[half, :, bass.ds(NPR + DQ * b, DQ)], src[:, :, DQ * hh:DQ * hh + DQ], ACT.Copy)\
                   .then_inc(do_used, 1)

        def attention_loads():
            vp = out["v_prompt"][0].rearrange("t h d -> t (h d)")
            full = P * (NT - 1)

            def load_v(m):
                ge_apart(sp, v_lo, 2 * m)
                sp.dma_start(VRAW[:, 0:NT - 1], vp[0:full, bass.ds(P * m, P)].rearrange("(t p) c -> p t c", p=P))\
                  .then_inc(v_loaded, 16)
                sp.dma_start(VRAW[0:LASTP, NT - 1], vp[full:NPR, bass.ds(P * m, P)]).then_inc(v_loaded, 16)

            def load_c(m, hh):
                ge_apart(sp, s_used, STEPS * m + NT * hh - NT)
                sp.dma_start(NEGC[:, hh], c_rows[bass.ds(2 * m + hh, 1)].to_broadcast([P, NPR]))\
                  .then_inc(c_loaded[hh], 16)

            sp.wait_ge(unit_done, U_O)
            sp.wait_ge(z_fin, 2 * KC)
            sp.wait_ge(kv_stored, 48 * 2 * KC)
            sp.wait_ge(c_stored, 16)
            sp.wait_ge(v_zero, 1)
            load_v(0)
            load_c(0, 0)
            def pair(m):
                load_c(m, 1)
                load_v(m + 1)
                load_c(m + 1, 0)
            pair(0)
            with sp.Fori(1, KC - 1) as m:
                pair(m)
            load_c(KC - 1, 1)

            def load_pages(cache, to, index, done):
                for g in range(NPAGE):
                    page = sp.value_load(PTAB[0:1, bass.ds(index + g, 1)], min_val=0,
                                         max_val=a["cache_k"].shape[0] - 1)
                    sp.dma_start(to[:, g], cache[bass.ds(page, 1)].rearrange("o t h d -> (o t) (h d)"))\
                      .then_inc(done, 16)

            sp.wait_ge(ring_free, PROMPT_GROUPS)
            sp.dma_start(PTAB[:, :], a["page_table"].rearrange("b g -> (b g)").rearrange("(o n) -> o n", o=1))\
              .then_inc(ids_loaded, 16)
            sp.dma_start(VPG[0:NS, 0], out["v_sample"].rearrange("b t h d -> (b t) (h d)")).then_inc(vn_loaded, 16)
            sp.wait_ge(ids_loaded, 16)
            with sp.Fori(0, DB * NPAGE) as x:
                page = sp.value_load(PTAB[0:1, bass.ds(x, 1)], min_val=0, max_val=a["cache_k"].shape[0] - 1)
                sp.dma_start(LPG[:, x], a["cache_logf"][bass.ds(page, 1)].rearrange("o t h -> (o t) h"))\
                  .then_inc(lp_loaded, 16)

            def pages(i, first=False):
                for c in range(2):
                    b = c + 2 * i
                    ge_apart(sp, dt_done, 4 * (b - 1))
                    load_pages(a["cache_k"], KPG[:, c], NPAGE * b, dk_loaded[c])
                    if first and c == 0:
                        sp.wait_ge(new_lo, 2)
                    ge_apart(sp, dv_lo, b)
                    load_pages(a["cache_v"], VPG, NPAGE * b, dv_loaded)
            pages(0, True)
            with sp.Fori(1, DB // 2) as i:
                pages(i)

        def attention_pool():
            pool.wait_ge(unit_done, U_O)
            pool.wait_ge(z_fin, 2 * KC)
            pool.wait_ge(k_kept, KC)
            pool.memset(VRAW[:, NT - 1], 0.0).then_inc(v_zero, 1)
            pool.memset(MASKF[:, :], 0.0).then_inc(p_const, 1)
            pool.wait_ge(p_const, 1)
            pool.affine_select(out=MASKF[:, :], in_=MASKF[:, :], compare_op=ALU.is_ge, fill=MASKED, base=0,
                               pattern=[[-1, P]], channel_multiplier=1).then_inc(p_const, 1)
            prep_pool(0, 0)
            prep_pool(0, 1)
            with pool.Fori(1, KC) as m:
                prep_pool(m, 0)
                prep_pool(m, 1)

            pool.wait_ge(ring_free, PROMPT_GROUPS)
            for t, x in ((QBH[:, :].bitcast(F32), 0.0), (QBL[:, :].bitcast(F32), 0.0), (CSF[:, :], 0.0), (EXF[:, :], 1.0),
                         (MW[:, :, :], MASKED), (MB[:, :, :], MASKED), (MBC[:, :, :], 0.0)):
                pool.memset(t, x).then_inc(d_const, 1)
            pool.wait_ge(d_const, 7)
            pool.affine_select(out=EXF[:, :], in_=EXF[:, :], compare_op=ALU.is_ge, fill=0.0, base=0,
                               pattern=[[1, HQ]], channel_multiplier=-DQ).then_inc(d_const, 1)
            pool.affine_select(out=MW[:, :, :], in_=MW[:, :, :], compare_op=ALU.is_ge, fill=0.0, base=-1,
                               pattern=[[DQ, NH], [1, DQ]], channel_multiplier=-1).then_inc(d_const, 1)
            pool.wait_ge(d_const, 9)
            pool.affine_select(out=EXF[:, :], in_=EXF[:, :], compare_op=ALU.is_ge, fill=0.0, base=DQ - 1,
                               pattern=[[-1, HQ]], channel_multiplier=DQ).then_inc(d_const, 1)
            pool.affine_select(out=MW[:, :, :], in_=MW[:, :, :], compare_op=ALU.is_ge, fill=0.0, base=0,
                               pattern=[[-DQ, NH], [0, DQ]], channel_multiplier=1).then_inc(d_const, 1)
            pool.wait_ge(d_mask, DB + 1)

            def mask_of(i):
                for c in range(2):
                    b = c + 2 * i
                    ge_apart(pool, ds_used, b - 1)
                    pool.tensor_copy(MBC[:, c, PAST:KEYS], MB[:, b]).then_inc(mb_ready, 1)
            mask_of(0)
            with pool.Fori(1, DB // 2) as i:
                mask_of(i)

        def attention_scalar():
            act.wait_ge(unit_done, U_O)
            act.wait_ge(z_fin, 2 * KC)
            act.wait_ge(p_const, 2)
            act.activation(MASK[:, :], MASKF[:, :], ACT.Copy).then_inc(p_round, 1)
            act.activation(IDR[:, :], ident[:, :], ACT.Copy).then_inc(p_round, 1)
            prep_act(0, 0, 0)
            prep_act(0, 0, 1)
            exp_logits(0, 0)
            exp_logits(0, 1)

            def body(m, first=False, last=False):
                for n in range(STEPS):
                    probs_hi(m, n)
                    if not last or n + 2 < STEPS:
                        exp_logits(m, n + 2)
                    if n == 0 and not first:
                        output_part(m - 1, STEPS - 1)
                    if n > 0:
                        output_part(m, n - 1)
                    if n in (1, 2):
                        prep_act(m, 1, n - 1)
                    if n in (10, 11) and not last:
                        prep_act(m + 1, 0, n - 10)

            body(0, first=True)
            with act.Fori(1, KC - 1) as m:
                body(m)
            body(KC - 1, last=True)
            output_part(KC - 1, STEPS - 1)

            act.wait_ge(ring_free, PROMPT_GROUPS)
            act.activation(KTH[:, :, PAST:KEYS], KS[:, :, NPR:TOK], ACT.Copy).then_inc(new_hi, 1)
            act.wait_ge(vn_loaded, 16)
            act.activation(VDH[:, :], VPG[0:NS, 0], ACT.Copy).then_inc(new_hi, 1)
            act.wait_ge(d_const, 11)
            act.activation(EX[:, :], EXF[:, :], ACT.Copy).then_inc(new_hi, 1)
            for g in range(4):
                act.wait_ge(past_done, g + 1)
                act.activation(CS[:, 2 * g:2 * g + 2, 0:PAST],
                               PS[0:NH, 4 + g % 2, :].rearrange("h (b k) -> h b k", b=2), ACT.Copy)\
                   .then_inc(past_kept, 1)
            act.activation(CS_NEW, LF[:, NPR:TOK].rearrange("h (b k) -> h b k", b=DB), ACT.Copy)\
               .then_inc(past_kept, 1)
            act.wait_ge(d_sums, DB)
            d_hi(0, 0)
            d_exp(0, 0)

            def pair(i, last=False):
                for c in range(2):
                    more = c == 0 or not last
                    if more:
                        d_hi(i + c, 1 - c)
                    d_values_hi(i, c)
                    d_probs_hi(i, c)
                    if more:
                        d_exp(i + c, 1 - c)
                    d_output(i, c)
            pair(0)
            with act.Fori(1, DB // 2 - 1) as i:
                pair(i)
            pair(DB // 2 - 1, True)

            act.wait_ge(do_used, 2 * DB)
            for m in range(KC):
                act.activation(HH[:, m], QS[:, m], ACT.Copy).then_inc(o_hi, 1)

        def attention_vector():
            dve.wait_ge(unit_done, U_O)
            dve.wait_ge(z_fin, 2 * KC)
            prep_dve(0, 0)
            max_logits(0, 0)
            max_logits(0, 1)

            def body(m, first=False, last=False):
                for n in range(STEPS):
                    if not last or n + 2 < STEPS:
                        max_logits(m, n + 2)
                    probs_lo(m, n)
                    inverse_sums(m, n)
                    if n == 0 and not first:
                        output_tile(m - 1, STEPS - 1)
                    if n == 1 and not first:
                        keep_output(m)
                    if n > 0:
                        output_tile(m, n - 1)
                    if n == 1:
                        prep_dve(m, 1)
                    if n == 10 and not last:
                        prep_dve(m + 1, 0)

            body(0, first=True)
            with dve.Fori(1, KC - 1) as m:
                body(m)
            body(KC - 1, last=True)
            output_tile(KC - 1, STEPS - 1)
            keep_output(KC)

            dve.wait_ge(new_hi, 1)
            dve.tensor_tensor(KTL[:, :, PAST:KEYS], KS[:, :, NPR:TOK], KTH[:, :, PAST:KEYS].bitcast(F32),
                              ALU.subtract).then_inc(new_lo, 1)
            dve.wait_ge(new_hi, 2)
            dve.tensor_tensor(VDL[:, :], VPG[0:NS, 0], VDH[:, :].bitcast(F32), ALU.subtract).then_inc(new_lo, 1)
            dve.wait_ge(d_const, 11)
            dve.tensor_reduce(M4[:, :], MW[:, :, :].rearrange("r h j -> r j h"), mybir.AxisListType.X, ALU.add)\
               .then_inc(d_mask, 1)
            dve.wait_ge(d_mask, 1)
            for b in range(DB):
                dve.tensor_copy(MB[:, b, DQ * b:DQ * b + DQ], M4[:, :]).then_inc(d_mask, 1)
            dve.wait_ge(past_kept, 5)
            for b in range(DB):
                dve.tensor_tensor_scan(CS[:, b], ones[0:NH, 0:1].bitcast(F32).to_broadcast([NH, KEYS]), CS[:, b],
                                       0.0, ALU.mult, ALU.add).then_inc(d_sums, 1)
            d_lo(0, 0)
            d_max(0, 0)
            d_norm(0, 0)

            def pair(i, last=False):
                for c in range(2):
                    more = c == 0 or not last
                    if more:
                        d_lo(i + c, 1 - c)
                    d_values_lo(i, c)
                    if more:
                        d_max(i + c, 1 - c)
                    d_probs_lo(i, c)
                    if more:
                        d_norm(i + c, 1 - c)
            pair(0)
            with dve.Fori(1, DB // 2 - 1) as i:
                pair(i)
            pair(DB // 2 - 1, True)
            for m in range(KC):
                dve.wait_ge(o_hi, m + 1)
                dve.tensor_tensor(HL[:, m], QS[:, m], HH[:, m].bitcast(F32), ALU.subtract).then_inc(o_lo, 1)

        def attention_tensor():
            pe.wait_ge(p_round, 2)
            logits(0, 0)
            logits(0, 1)

            def body(m, first=False, last=False):
                for n in range(STEPS):
                    if not last or n + 2 < STEPS:
                        logits(m, n + 2)
                    turn_probs(m, n)
                    if n == 1 and not first:
                        turn_output(m)
                    if n == 0 and not first:
                        weigh_values(m - 1, STEPS - 1)
                    if n > 0:
                        weigh_values(m, n - 1)

            body(0, first=True)
            with pe.Fori(1, KC - 1) as m:
                body(m)
            body(KC - 1, last=True)
            weigh_values(KC - 1, STEPS - 1)
            turn_output(KC)

            pe.wait_ge(lp_loaded, 16 * DB * NPAGE)
            pe.wait_ge(ring_free, PROMPT_GROUPS)
            for g in range(4):
                ge(pe, past_kept, g - 1)
                for x in range(4):
                    mm = pe.transpose(PS[0:NH, 4 + g % 2, P * x:P * x + P], LPG[:, 4 * g + x], ident[:, :])
                mm.then_inc(past_done, 1)
            pe.wait_ge(new_lo, 2)
            pe.wait_ge(new_hi, 3)
            d_turn_keys(0, 0)
            d_logits(0, 0)

            def pair(i, last=False):
                for c in range(2):
                    if c == 0 or not last:
                        d_turn_keys(i + c, 1 - c)
                        d_logits(i + c, 1 - c)
                    d_turn_probs(i, c)
                    d_weigh(i, c)
            pair(0)
            with pe.Fori(1, DB // 2 - 1) as i:
                pair(i)
            pair(DB // 2 - 1, True)

        def o_ready(k):
            pe.wait_ge(o_lo, k + 1)

        def y_tensor():
            for t in range(NT):
                tok, rows = sides(t)
                for c in range(2):
                    n = AX_Y + 2 * t + c
                    pe.wait_ge(aux_read, n - 1)
                    if t == 0:
                        pe.wait_ge(unit_read, N_UNITS - 4 + 4 * c)
                    for k in range(4):
                        mm = pe.transpose(PS[0:rows, 6 + n % 2, P * k:P * k + P], ACC[:, 4 * c + k, tok:tok + rows],
                                          ident[:, :])
                    mm.then_inc(aux_done, 1)

        def y_scalar():
            for t in range(NT):
                rows = sides(t)[1]
                ge(act, y_stored[t % 4], 16 * (t // 4))
                for c in range(2):
                    n = AX_Y + 2 * t + c
                    act.wait_ge(aux_done, n + 1)
                    act.activation(YO[0:rows, t % 4, 512 * c:512 * c + 512], PS[0:rows, 6 + n % 2, :], ACT.Copy)\
                       .then_inc(aux_read, 1)

        def y_vector():
            pass

        def store_y():
            y = out["y_prompt"][0]
            for t in range(NT):
                sp.wait_ge(aux_read, AX_Y + 2 * t + 2)
                if t == 0:
                    sp.dma_start(y[0:P - META], YO[META:P, 0]).then_inc(y_stored[0], 16)
                elif t < NT - 1:
                    sp.dma_start(y[P * t - META:P * t - META + P], YO[:, t % 4]).then_inc(y_stored[t % 4], 16)
                else:
                    sp.dma_start(y[SEQ - LASTP:SEQ], YO[0:LASTP, t % 4]).then_inc(y_stored[t % 4], 16)
                    sp.dma_start(out["y_sample"].rearrange("b t d -> (b t) d"), YO[LASTP:LAST, t % 4])\
                      .then_inc(y_stored[t % 4], 16)
            sp.wait_ge(y_stored[0], 16 * 4)
            for x in range(1, 4):
                sp.wait_ge(y_stored[x], 16 * 2)
            sp.wait_ge(kv_stored, 48 * 2 * KC)
            sp.wait_ge(logf_stored, 48)
            sp.wait_ge(c_stored, 16)
            sp.wait_ge(conv_stored, 32)

        block = ctx.enter_context(nc.Block())

        MIX_COL = (1, 2, 0)
        HID = [KC, 2 * KC + FF_BLK * KC - KC]

        @block.sync
        def _(sync):
            xs = a["x_sample"].rearrange("b t d -> (b t) d")
            xp = a["x_prompt"][0]
            for g, x in ((G_MIX[0], a["norm_mix"].rearrange("l (k p) -> (l k) p", p=P)),
                         (G_MLP[0], a["norm_mlp"].rearrange("l (k p) -> (l k) p", p=P)),
                         (G_KV, a["norm_kv"].rearrange("(k p) -> k p", p=P)),
                         (G_CONV, a["conv_w"][0].rearrange("j (k p) -> (j k) p", p=P))):
                sp.dma_start(VIN[g:g + x.shape[0], :], x).then_inc(vec_loaded, 16)
            for g, x in ((G_KN, a["k_norm"].rearrange("(o d) -> o d", o=1)), (G_QN, a["q_norm"])):
                for half in range(2):
                    sp.dma_start(VIN[g:g + 1, half * HD:(half + 1) * HD], x).then_inc(vec_loaded, 16)
            sp.dma_start(STI[:, :], a["state_conv"][0].rearrange("b j d -> (b j) d")).then_inc(state_loaded, 16)
            sp.dma_start(IN[0:META, 0], a["meta_tokens"]).then_inc(in_loaded[0], 16)
            sp.dma_start(IN[META:P, 0], xp[0:P - META]).then_inc(in_loaded[0], 16)
            for t in range(1, NT - 1):
                sp.dma_start(IN[:, t], xp[P * t - META:P * t - META + P]).then_inc(in_loaded[t], 16)
            sp.dma_start(IN[0:LASTP, NT - 1], xp[SEQ - LASTP:SEQ]).then_inc(in_loaded[NT - 1], 16)
            sp.dma_start(IN[LASTP:LAST, NT - 1], xs).then_inc(in_loaded[NT - 1], 16)

            def mixer(i):
                for m2 in range(2):
                    for j in range(3):
                        load_unit(a["conv_w_in"][0], 0, MIX_COL[j] * D + P * m2 + 2 * P * i,
                                  3 * m2 + j, i, 6)

            def columns(u0, w, col0=0, row0=0, turn=0):
                with sp.Fori(0, KC // 2) as i:
                    for c in range(2):
                        load_unit(w, row0, col0 + P * c + 2 * P * i, u0 + c, turn + i)

            def mlp(l):
                with sp.Fori(0, FF_BLK) as b:
                    columns(U_MLP[l], a["mlp_w1"][l], D * b, 0, KC * b)
                    columns(U_MLP[l] + KC, a["mlp_w2"][l], 0, KC * b, KC * b)

            mixer(0)
            sp.dma_start(BF[:, :], a["b_f"].rearrange("(n o) -> n o", o=1)).then_inc(bf_loaded, 16)
            sp.dma_start(WFR[:, :, :], a["w_f"].rearrange("(k p) n -> p k n", p=P)).then_inc(gate_w_loaded, 16)
            with sp.Fori(1, KC // 2) as i:
                mixer(i)
            columns(U_OUT, a["conv_w_out"][0])
            sp.wait_ge(aux_read, AX_CONV + 2)
            sp.dma_start(out["conv_prompt"][0, 0], CO[0:CW - 1, :]).then_inc(conv_stored, 16)
            sp.dma_start(out["conv_sample"][0].rearrange("b j d -> (b j) d"),
                         CO[CW - 1:(DB + 1) * (CW - 1), :]).then_inc(conv_stored, 16)
            mlp(0)
            columns(U_K, a["w_kv"])
            columns(U_V, a["w_kv"], D)
            columns(U_Q, a["w_q"][0])
            for c in range(2):
                load_unit(a["w_o"][0], 0, P * c, U_O + c)
            attention_loads()
            with sp.Fori(1, KC // 2) as i:
                for c in range(2):
                    load_unit(a["w_o"][0], 0, P * c + 2 * P * i, U_O + c, i)
            mlp(1)
            store_y()

        @block.gpsimd
        def _(gpsimd):
            pool.memset(ident[:, :], 0.0).then_inc(zero_ready, 1)
            pool.wait_ge(zero_ready, 1)
            pool.affine_select(out=ident[:, :], in_=ident[:, :], compare_op=ALU.not_equal, fill=1.0, base=0,
                               pattern=[[-1, P]], channel_multiplier=1).then_inc(const_ready, 1)
            pool.memset(ACC[:, :, TOK:T], 0.0).then_inc(const_ready, 1)

            def sums(f):
                residual_sum(f, 0)
                residual_sum(f, 1)
                with pool.Fori(1, KC // 2) as i:
                    for c in range(2):
                        residual_sum(f, 2 * i + c)

            sums(0)
            sums(1)
            sums(2)

            def head_squares(u, par, n):
                pool.wait_ge(unit_read, u + 1)
                ge(pool, z_fin, n)
                pool.tensor_tensor(T1[:, :], KW[:, par], KW[:, par], ALU.mult).then_inc(z_sq, 1)

            for u0, n0 in ((U_K, 0), (U_Q, KC)):
                head_squares(u0, 0, n0)
                head_squares(u0 + 1, 1, n0 + 1)
                with pool.Fori(1, KC // 2) as i:
                    for c in range(2):
                        head_squares(u0 + c + 2 * i, c, n0 + c + 2 * i)
            attention_pool()
            sums(3)

        @block.scalar
        def _(scalar):
            act.wait_ge(const_ready, 6)
            round_unit(0)
            round_unit(1)
            for t in range(NT):
                tok, rows = sides(t)
                for c in range(2):
                    n = AX_IN + 2 * t + c
                    act.wait_ge(aux_done, n + 1)
                    act.activation(ACC[:, 4 * c:4 * c + 4, tok:tok + rows],
                                   PS[:, 6 + n % 2, 0:4 * rows].rearrange("p (k r) -> p k r", r=rows),
                                   ACT.Copy).then_inc(aux_read, 1)
            act.wait_ge(aux_done, AX_VEC + 1)
            act.activation(vecs[:, :], PS[:, 6 + AX_VEC % 2, 0:N_VEC], ACT.Copy).then_inc(aux_read, 1)
            act.wait_ge(aux_done, AX_VEC + 2)
            act.activation(CST[:, :, :].rearrange("p k s -> p (k s)"),
                           PS[:, 6 + (AX_VEC + 1) % 2, 0:KC * DB * (CW - 1)], ACT.Copy).then_inc(aux_read, 1)
            act.wait_ge(aux_read, AX_VEC + 2)
            residual_hi(0, 0, 0)
            with act.Fori(1, KC) as m:
                residual_hi(0, m, 0)
            rms_split_hi(0)

            def hid_hi_of(n, j):
                act.wait_ge(h_raw, n + 1)
                act.activation(HH[:, j], T1[:, :], ACT.Copy).then_inc(hid_hi, 1)

            def mixer(i, first=False):
                for m2 in range(2):
                    for j in range(3):
                        round_unit(3 * m2 + j + 2, i, 6)
                        if first and m2 == 0 and j == 0:
                            rms_root(0)
                    hid_hi_of(2 * i + m2, 2 * i + m2)

            mixer(0, True)
            with act.Fori(1, KC // 2) as i:
                mixer(i)

            def residual_turns(u0, split, f, turn=0, prefetch=True):
                def one(i, c):
                    round_unit(u0 + c + 2, turn + i)
                    act.wait_ge(unit_read, u0 + c + 2 * (turn + i) + 1)
                    residual_hi(split, c + 2 * i, f)
                one(0, 0)
                one(0, 1)
                with act.Fori(1, KC // 2) as i:
                    one(i, 0)
                    one(i, 1)

            for c in range(2):
                n = AX_CONV + c
                act.wait_ge(aux_done, n + 1)
                act.activation(CO[:, 512 * c:512 * c + 512], PS[0:(DB + 1) * (CW - 1), 6 + n % 2, :],
                               ACT.Copy).then_inc(aux_read, 1)
            act.wait_ge(gate_w_loaded, 16)
            act.activation(WFH[:, :, :], WFR[:, :, :], ACT.Copy).then_inc(gate_hi, 1)
            residual_turns(U_OUT, 1, 1)

            def mlp(l, s):
                U = U_MLP[l]
                rms_split_hi(s)

                def up(b, i, c, root=False):
                    round_unit(U + c + 2, KC * b + i)
                    if root:
                        rms_root(s)
                    hid_hi_of(HID[l] + KC * b + c + 2 * i, c + 2 * i)

                def down(b, i, c):
                    round_unit(U + KC + c + 2, KC * b + i)

                up(0, 0, 0, True)
                up(0, 0, 1)
                with act.Fori(1, KC // 2) as i:
                    up(0, i, 0)
                    up(0, i, 1)
                with act.Fori(0, KC // 2) as i:
                    down(0, i, 0)
                    down(0, i, 1)
                with act.Fori(1, FF_BLK - 1) as b:
                    with act.Fori(0, KC // 2) as i:
                        up(b, i, 0)
                        up(b, i, 1)
                    with act.Fori(0, KC // 2) as i:
                        down(b, i, 0)
                        down(b, i, 1)
                b = FF_BLK - 1
                with act.Fori(0, KC // 2) as i:
                    up(b, i, 0)
                    up(b, i, 1)
                if l == 0:
                    residual_turns(U + KC + 2 * KC * b, 2, 2)
                else:
                    with act.Fori(0, KC // 2 - 1) as i:
                        down(b, i, 0)
                        down(b, i, 1)

            mlp(0, 1)

            rms_split_hi(2)

            def head_hi(n):
                act.wait_ge(z_sq, n + 1)
                ge(act, z_fin, n)
                act.activation(T2R[:, :], T1[:, :], ACT.Copy).then_inc(z_hi, 1)

            def head_root(n):
                for g in range(G):
                    act.wait_ge(aux_done, n[1] + g + 1)
                    act.activation(T2[:, g * GW:(g + 1) * GW], PS[:, 6 + (n[0] + g) % 2, 0:GW], ACT.Sqrt,
                                   scale=1.0 / HD, bias=epst[:, 0:1]).then_inc(aux_read, 1)

            def keep_k(i, c):
                m, n = c + 2 * i, ax(AX_K + G + 6 * c, 12, i)
                act.wait_ge(z_fin, m + 1)
                act.activation(KS[:, m], KW[:, c % 2], ACT.Copy).then_inc(k_kept, 1)
                keep_tokens(n, m)
                store_tokens(n, out["k_prompt"], out["k_sample"], m)

            def keep_v(i, c):
                m, n = c + 2 * i, ax(AX_V + 3 * c, 6, i)
                keep_tokens(n, KC + m)
                store_tokens(n, out["v_prompt"], out["v_sample"], m)

            round_unit(U_K + 2)
            rms_root(2)
            for g in range(G):
                act.wait_ge(aux_done, AX_F + g + 1)
                act.activation(LF[:, g * GW:(g + 1) * GW], PS[0:NH, 6 + (AX_F + g) % 2, 0:GW],
                               ACT.Copy).then_inc(aux_read, 1)
            head_hi(0)
            head_root(ax(AX_K, 0, 0))
            round_unit(U_K + 3)
            keep_k(0, 0)
            head_hi(1)
            head_root(ax(AX_K + 6, 0, 0))
            with act.Fori(1, KC // 2) as i:
                round_unit(U_K + 2, i)
                keep_k(i - 1, 1)
                head_hi(2 * i)
                head_root(ax(AX_K, 12, i))
                round_unit(U_K + 3, i)
                keep_k(i, 0)
                head_hi(2 * i + 1)
                head_root(ax(AX_K + 6, 12, i))
            round_unit(U_V + 2)
            keep_k(KC // 2 - 1, 1)
            keep_v(0, 0)
            round_unit(U_V + 3)
            act.wait_ge(gate_step, 3)
            act.activation(ZE[:, :], ZN[:, :], ACT.Exp).then_inc(gate_act, 1)
            act.wait_ge(gate_step, 4)
            act.activation(LF[:, :], ZU[:, :], ACT.Ln).then_inc(gate_act, 1)
            keep_v(0, 1)
            with act.Fori(1, KC // 2 - 1) as i:
                for c in range(2):
                    round_unit(U_V + c + 2, i)
                    keep_v(i, c)
            i = KC // 2 - 1
            round_unit(U_V + 2, i)
            keep_v(i, 0)
            round_unit(U_V + 3, i)
            act.wait_ge(unit_done, U_Q)
            with act.Fori(0, KC) as m:
                residual_hi(3, m)
            keep_v(i, 1)
            act.wait_ge(aux_done, AX_LF + 1)
            b = 6 + AX_LF % 2
            act.activation(LT[:, 0:NT - 1], PS[:, b, 0:NH * (NT - 1)].rearrange("p (t h) -> p t h", h=NH),
                           ACT.Copy).then_inc(lt_kept, 1)
            act.activation(LT[0:LAST, NT - 1], PS[0:LAST, b, NH * (NT - 1):NH * NT], ACT.Copy)\
               .then_inc(aux_read, 1)
            act.wait_ge(lt_kept, 1)
            act.wait_ge(aux_read, AX_LF + 1)
            full = P * (NT - 1)
            act.dma_start(out["logf_prompt"][0, 0:full].rearrange("(t p) h -> p t h", p=P), LT[:, 0:NT - 1])\
               .then_inc(logf_stored, 16)
            act.dma_start(out["logf_prompt"][0, full:NPR], LT[0:LASTP, NT - 1]).then_inc(logf_stored, 16)
            act.dma_start(out["logf_sample"].rearrange("b t h -> (b t) h"), LT[LASTP:LAST, NT - 1])\
               .then_inc(logf_stored, 16)
            act.wait_ge(gate_step, 9)
            act.dma_start(c_rows, C8[:, :]).then_inc(c_stored, 16)

            def q_turn(i):
                for c in range(2):
                    round_unit(U_Q + c + 2, i)
                    head_hi(KC + c + 2 * i)
                    head_root(ax(AX_Q + 3 * c, 6, i))
            with act.Fori(0, KC // 2) as i:
                q_turn(i)

            attention_scalar()

            residual_turns(U_O, 4, 3)
            mlp(1, 3)
            y_scalar()

        @block.vector
        def _(vector):
            dve.memset(epst[:, :], EPS).then_inc(const_ready, 1)
            dve.memset(ones[:, :].bitcast(F32), 1.0).then_inc(const_ready, 1)
            dve.memset(heads1[:, :].bitcast(F32), 0.0).then_inc(heads_zero, 1)
            dve.wait_ge(heads_zero, 1)
            for h in range(2):
                s = slice(h * HD, (h + 1) * HD)
                dve.memset(heads1[s, s].bitcast(F32), 1.0).then_inc(const_ready, 1)
            cut_unit(0)
            cut_unit(1)
            with dve.Fori(0, KC) as m:
                residual_lo(0, m)
            rms_split_lo(0)

            def scaled(c, i, stride, to, by):
                u = c + stride * i
                dve.wait_ge(unit_done, u + 1)
                dve.tensor_tensor(banks(to), result(c), banks(by), ALU.mult).then_inc(unit_read, 1)

            def hid_lo_of(n, j):
                dve.wait_ge(hid_hi, n + 1)
                dve.tensor_tensor(HL[:, j], T1[:, :], HH[:, j].bitcast(F32), ALU.subtract).then_inc(hid_lo, 1)

            T1P, T1S = T1[:, 0:NPR], T1[:, NPR:TOK].rearrange("p (b t) -> p b t", b=DB)
            RP, RS = R[:, 0:NPR], R[:, NPR:TOK].rearrange("p (b t) -> p b t", b=DB)

            def mixer(i, first=False):
                for m2 in range(2):
                    m, c = 2 * i + m2, 3 * m2
                    cut_unit(c + 2, i, 6)
                    if first and m2 == 0:
                        rms_inverse(0)
                    ge(dve, hid_lo, m)
                    scaled(c, i, 6, T1[:, :], R[:, :])
                    dve.wait_ge(unit_read, c + 6 * i + 1)
                    cut_unit(c + 3, i, 6)
                    scaled(c + 1, i, 6, T1[:, :], T1[:, :])
                    dve.wait_ge(unit_read, c + 1 + 6 * i + 1)
                    dve.tensor_tensor(UP[:, CW - 1:CW - 1 + NPR], T1P, RP, ALU.mult).then_inc(u_ready, 1)
                    dve.tensor_tensor(US[:, :, CW - 1:], T1S, RS, ALU.mult).then_inc(u_ready, 1)
                    dve.memset(UP[:, 0:CW - 1], 0.0).then_inc(u_ready, 1)
                    dve.tensor_copy(US[:, :, 0:CW - 1], CST[:, m].rearrange("p (b j) -> p b j", b=DB))\
                       .then_inc(u_ready, 1)
                    dve.wait_ge(u_ready, 4 * (m + 1))
                    dve.tensor_copy(UL[:, m, 0:CW - 1], UP[:, NPR:NPR + CW - 1]).then_inc(u_last, 1)
                    dve.tensor_copy(UL[:, m, CW - 1:].rearrange("p (b j) -> p b j", b=DB),
                                    US[:, :, DQ:DQ + CW - 1]).then_inc(u_last, 1)
                    for j in range(CW):
                        tap = vecs[:, bass.ds(G_CONV + KC * j + m, 1)]
                        src = ((T1P, UP[:, j:j + NPR]), (T1S, US[:, :, j:j + DQ]))
                        if j:
                            dve.wait_ge(conv_step, 2 * CW * m + 2 * j)
                        for to, x in src:
                            if j == 0:
                                dve.tensor_scalar(to, x, tap, None, ALU.mult).then_inc(conv_step, 1)
                            else:
                                dve.scalar_tensor_tensor(to, x, tap, to, ALU.mult, ALU.add)\
                                   .then_inc(conv_step, 1)
                    cut_unit(c + 4, i, 6)
                    dve.wait_ge(conv_step, 2 * CW * (m + 1))
                    scaled(c + 2, i, 6, T1[:, :], T1[:, :])
                    dve.wait_ge(unit_read, c + 2 + 6 * i + 1)
                    dve.tensor_tensor(T1[:, :], T1[:, :], R[:, :], ALU.mult).then_inc(h_raw, 1)
                    hid_lo_of(m, m)

            mixer(0, True)
            with dve.Fori(1, KC // 2) as i:
                mixer(i)

            dve.wait_ge(gate_hi, 1)
            dve.tensor_tensor(WFL[:, :, :], WFR[:, :, :], WFH[:, :, :].bitcast(F32), ALU.subtract)\
               .then_inc(gate_lo, 1)

            def add_residual(c, i, m):
                u = c + 2 * i
                dve.wait_ge(unit_done, u + 1)
                dve.tensor_tensor(banks(ACC[:, m]), result(c), banks(ACC[:, m]), ALU.add).then_inc(unit_read, 1)

            def residual_turns(u0, split):
                with dve.Fori(0, KC // 2) as i:
                    for c in range(2):
                        cut_unit(u0 + c + 2, i)
                        add_residual(u0 + c, i, c + 2 * i)
                        residual_lo(split, c + 2 * i)

            residual_turns(U_OUT, 1)

            def mlp(l, s):
                U = U_MLP[l]
                rms_split_lo(s)

                def up(b, i, c, inverse=False):
                    n, u = HID[l] + KC * b + c + 2 * i, U + c + 2 * (KC * b + i)
                    cut_unit(U + c + 2, KC * b + i)
                    if inverse:
                        rms_inverse(s)
                    dve.wait_ge(hid_lo, n)
                    dve.wait_ge(unit_done, u + 1)
                    dve.scalar_tensor_tensor(banks(T1[:, :]), result(c), 0.0, banks(R[:, :]), ALU.max,
                                             ALU.mult).then_inc(unit_read, 1)
                    dve.wait_ge(unit_read, u + 1)
                    dve.tensor_tensor(T1[:, :], T1[:, :], T1[:, :], ALU.mult).then_inc(h_raw, 1)
                    hid_lo_of(n, c + 2 * i)

                def down(b, i, c):
                    cut_unit(U + KC + c + 2, KC * b + i)
                    add_residual(U + KC + c, KC * b + i, c + 2 * i)

                up(0, 0, 0, True)
                up(0, 0, 1)
                with dve.Fori(1, KC // 2) as i:
                    up(0, i, 0)
                    up(0, i, 1)
                with dve.Fori(0, KC // 2) as i:
                    down(0, i, 0)
                    down(0, i, 1)
                with dve.Fori(1, FF_BLK - 1) as b:
                    with dve.Fori(0, KC // 2) as i:
                        up(b, i, 0)
                        up(b, i, 1)
                    with dve.Fori(0, KC // 2) as i:
                        down(b, i, 0)
                        down(b, i, 1)
                b = FF_BLK - 1
                with dve.Fori(0, KC // 2) as i:
                    up(b, i, 0)
                    up(b, i, 1)
                if l == 0:
                    residual_turns(U + KC + 2 * KC * b, 2)
                else:
                    with dve.Fori(0, KC // 2 - 1) as i:
                        down(b, i, 0)
                        down(b, i, 1)
                    down(b, KC // 2 - 1, 0)
                    down(b, KC // 2 - 1, 1)

            mlp(0, 1)

            rms_split_lo(2)

            def head_norm(n, sums, par, gain, to):
                dve.wait_ge(z_hi, n + 1)
                dve.tensor_tensor(T1R[:, :], T1[:, :], T2R[:, :].bitcast(F32), ALU.subtract).then_inc(z_lo, 1)
                dve.wait_ge(aux_read, sums[1] + G)
                dve.reciprocal(T2[:, 0:T], T2[:, 0:T]).then_inc(z_inv, 1)
                dve.wait_ge(z_inv, n + 1)
                dve.scalar_tensor_tensor(to, KW[:, par], vecs[:, gain:gain + 1], T2[:, 0:T],
                                         ALU.mult, ALU.mult).then_inc(z_fin, 1)

            def k_turn(i, c, inverse=False, first=False):
                cut_unit(U_K + c + 2, i)
                if inverse:
                    rms_inverse(2)
                    dve.wait_ge(conv_stored, 32)
                if not first:
                    dve.wait_ge(aux_read, AX_K + 3 + 6 * (c - 2) + 12 * i + G)
                scaled(U_K + c, i, 2, KW[:, c], R[:, :])
                head_norm(c + 2 * i, ax(AX_K + 6 * c, 12, i), c, G_KN, KW[:, c])

            k_turn(0, 0, True, True)
            k_turn(0, 1, False, True)
            with dve.Fori(1, KC // 2) as i:
                k_turn(i, 0)
                k_turn(i, 1)
            for c in range(2):
                cut_unit(U_V + c + 2)
                dve.wait_ge(aux_read, AX_K + 3 + 6 * (KC - 2 + c) + G)
                scaled(U_V + c, 0, 2, KW[:, c], R[:, :])
            dve.wait_ge(bf_loaded, 16)
            dve.wait_ge(aux_read, AX_F + G)
            dve.tensor_tensor(Z[:, :], LF[:, :], R[0:NH, :], ALU.mult).then_inc(gate_step, 1)
            dve.wait_ge(gate_step, 1)
            dve.tensor_scalar(Z[:, :], Z[:, :], BF[:, 0:1], None, ALU.add).then_inc(gate_step, 1)
            dve.wait_ge(gate_step, 2)
            dve.scalar_tensor_tensor(ZN[:, :], Z[:, :], -1.0, Z[:, :], ALU.mult, ALU.min).then_inc(gate_step, 1)
            dve.wait_ge(gate_act, 1)
            dve.tensor_scalar(ZU[:, :], ZE[:, :], 1.0, None, ALU.add).then_inc(gate_step, 1)
            dve.wait_ge(gate_act, 2)
            dve.scalar_tensor_tensor(ZU[:, :], ZU[:, :], 1.0, ZE[:, :], ALU.subtract, ALU.subtract)\
               .then_inc(gate_step, 1)
            dve.wait_ge(gate_step, 5)
            dve.tensor_tensor(LF[:, :], LF[:, :], ZU[:, :], ALU.subtract).then_inc(gate_step, 1)
            dve.wait_ge(gate_step, 6)
            dve.scalar_tensor_tensor(LF[:, :], Z[:, :], 0.0, LF[:, :], ALU.min, ALU.subtract).then_inc(gate_step, 1)
            dve.wait_ge(gate_step, 7)
            dve.tensor_tensor_scan(C8[:, :], ones[0:NH, 0:1].bitcast(F32).to_broadcast([NH, NPR]), LF[:, 0:NPR],
                                   0.0, ALU.mult, ALU.add).then_inc(gate_step, 1)
            dve.wait_ge(gate_step, 8)
            dve.tensor_scalar(C8[:, :], C8[:, :], -1.0 / SCALE, None, ALU.mult).then_inc(gate_step, 1)
            with dve.Fori(1, KC // 2) as i:
                for c in range(2):
                    cut_unit(U_V + c + 2, i)
                    dve.wait_ge(aux_read, AX_V + 3 * (c - 2) + 6 * i + G)
                    scaled(U_V + c, i, 2, KW[:, c], R[:, :])
            dve.wait_ge(unit_done, U_Q)
            with dve.Fori(0, KC) as m:
                residual_lo(3, m)

            def q_turn(i, c):
                cut_unit(U_Q + c + 2, i)
                dve.wait_ge(aux_read, AX_V + 3 * KC)
                scaled(U_Q + c, i, 2, KW[:, c], R[:, :])
                head_norm(KC + c + 2 * i, ax(AX_Q + 3 * c, 6, i), c, G_QN, QS[:, c + 2 * i])

            q_turn(0, 0)
            q_turn(0, 1)
            dve.wait_ge(logf_stored, 48)
            dve.wait_ge(c_stored, 16)
            with dve.Fori(1, KC // 2) as i:
                q_turn(i, 0)
                q_turn(i, 1)

            attention_vector()

            residual_turns(U_O, 4)
            mlp(1, 3)
            y_vector()

        @block.tensor
        def _(tensor):
            pe.wait_ge(const_ready, 6)
            for t in range(NT):
                tok, rows = sides(t)
                pe.wait_ge(in_loaded[t], 16 if 0 < t < NT - 1 else 32)
                for c in range(2):
                    n = AX_IN + 2 * t + c
                    ge(pe, aux_read, n - 1)
                    for k in range(4):
                        mm = pe.transpose(PS[:, 6 + n % 2, k * rows:(k + 1) * rows],
                                          IN[0:rows, t, P * (4 * c + k):P * (4 * c + k + 1)],
                                          ident[0:rows, 0:rows])
                    mm.then_inc(aux_done, 1)
            pe.wait_ge(vec_loaded, 16 * 8)
            pe.wait_ge(aux_read, AX_VEC - 1)
            pe.transpose(PS[:, 6 + AX_VEC % 2, 0:N_VEC], VIN[:, :], ident[0:N_VEC, 0:N_VEC]).then_inc(aux_done, 1)
            pe.wait_ge(state_loaded, 16)
            pe.wait_ge(aux_read, AX_VEC)
            ns = DB * (CW - 1)
            for k in range(KC):
                mm = pe.transpose(PS[:, 6 + (AX_VEC + 1) % 2, k * ns:(k + 1) * ns], STI[:, P * k:P * (k + 1)],
                                  ident[0:ns, 0:ns])
            mm.then_inc(aux_done, 1)

            def mixer(i, first=False):
                for c in range(6):
                    unit(c, i, 6, ready=x_ready(0) if first and c == 0 else None)
                    if first and c == 0:
                        rms_sums(0)

            mixer(0, True)
            with pe.Fori(1, KC // 2) as i:
                mixer(i)

            def eight(u0, turn=0, hi=XH, lo=XL, ready=None, after=None):
                unit(u0, turn, 2, hi, lo, ready)
                if after:
                    after()
                unit(u0 + 1, turn, 2, hi, lo)
                with pe.Fori(1, KC // 2) as i:
                    unit(u0, turn + i, 2, hi, lo)
                    unit(u0 + 1, turn + i, 2, hi, lo)

            def hid_ready(n):
                return lambda k: pe.wait_ge(hid_lo, n + k + 1)

            pe.wait_ge(u_last, 2 * KC)
            for c in range(2):
                n = AX_CONV + c
                pe.wait_ge(aux_read, n - 1)
                for k in range(4):
                    mm = pe.transpose(PS[0:(DB + 1) * (CW - 1), 6 + n % 2, P * k:P * (k + 1)],
                                      UL[:, 4 * c + k, :], ident[:, :])
                mm.then_inc(aux_done, 1)
            eight(U_OUT, 0, HH, HL, hid_ready(0))

            def mlp(l, split, s):
                U = U_MLP[l]
                eight(U, 0, XH, XL, x_ready(split), lambda: rms_sums(s))
                eight(U + KC, 0, HH, HL, hid_ready(HID[l]))
                with pe.Fori(1, FF_BLK) as b:
                    eight(U, KC * b)
                    eight(U + KC, KC * b, HH, HL, hid_ready(HID[l] + KC * b))

            mlp(0, 1, 1)

            def head_sums(n, z):
                return lambda: column_sums(n, heads1, lambda: pe.wait_ge(z_lo, z + 1))

            def turn_k(i, c):
                def f():
                    pe.wait_ge(z_fin, c + 2 * i + 1)
                    turn_tokens(c % 2, ax(AX_K + G + 6 * c, 12, i))
                return f

            def turn_v(i, c):
                def f():
                    pe.wait_ge(unit_read, U_V + c + 2 * i + 1)
                    turn_tokens(c % 2, ax(AX_V + 3 * c, 6, i))
                return f

            unit(U_K, ready=x_ready(2))
            rms_sums(2)
            pe.wait_ge(gate_lo, 1)
            for g in range(G):
                n = AX_F + g
                pe.wait_ge(aux_read, n - 1)
                for k in range(KC):
                    for j, (w, x) in enumerate(((WFH, XH), (WFH, XL), (WFL, XH))):
                        mm = pe.matmul(PS[0:NH, 6 + n % 2, 0:GW], w[:, k], x[:, k, g * GW:(g + 1) * GW],
                                       start=(k == 0 and j == 0), stop=(k == KC - 1 and j == 2))
                mm.then_inc(aux_done, 1)
            unit(U_K + 1, mid={4: head_sums(ax(AX_K, 0, 0), 0)})
            with pe.Fori(1, KC // 2) as i:
                unit(U_K, i, mid={2: turn_k(i - 1, 0), 4: head_sums(ax(AX_K - 6, 12, i), 2 * i - 1)})
                unit(U_K + 1, i, mid={2: turn_k(i - 1, 1), 4: head_sums(ax(AX_K, 12, i), 2 * i)})
            last = KC // 2 - 1
            unit(U_V, mid={2: turn_k(last, 0), 4: head_sums(ax(AX_K + 6 * (KC - 1), 0, 0), KC - 1)})
            unit(U_V + 1, mid={2: turn_k(last, 1), 4: turn_v(0, 0)})
            with pe.Fori(1, KC // 2) as i:
                unit(U_V, i, mid={4: turn_v(i - 1, 1)})
                unit(U_V + 1, i, mid={4: turn_v(i, 0)})

            def turn_logf():
                turn_v(last, 1)()
                pe.wait_ge(gate_step, 7)
                pe.wait_ge(aux_read, AX_LF - 1)
                for t in range(NT):
                    tok, rows = sides(t)
                    mm = pe.transpose(PS[0:rows, 6 + AX_LF % 2, NH * t:NH * t + NH], LF[:, tok:tok + rows],
                                      ident[0:NH, 0:NH])
                mm.then_inc(aux_done, 1)

            unit(U_Q, ready=x_ready(3), mid={4: turn_logf})
            unit(U_Q + 1, mid={4: head_sums(ax(AX_Q, 0, 0), KC)})
            with pe.Fori(1, KC // 2) as i:
                unit(U_Q, i, mid={4: head_sums(ax(AX_Q - 3, 6, i), KC + 2 * i - 1)})
                unit(U_Q + 1, i, mid={4: head_sums(ax(AX_Q, 6, i), KC + 2 * i)})
            head_sums(ax(AX_Q + 3 * (KC - 1), 0, 0), 2 * KC - 1)()

            attention_tensor()

            eight(U_O, 0, HH, HL, o_ready)
            mlp(1, 4, 3)
            y_tensor()


_OUTS = (("y_prompt", (1, SEQ, D)), ("y_sample", (DB, DQ, D)), ("k_prompt", (1, NPR, NH, HD)),
         ("v_prompt", (1, NPR, NH, HD)), ("logf_prompt", (1, NPR, NH)), ("conv_prompt", (1, 1, CW - 1, D)),
         ("k_sample", (DB, DQ, NH, HD)), ("v_sample", (DB, DQ, NH, HD)), ("logf_sample", (DB, DQ, NH)),
         ("conv_sample", (1, DB, CW - 1, D)))


def kernel(**inputs):
    import concourse.bacc as bacc
    from concourse.bass_utils import run_bass_kernel_spmd

    nc = bacc.Bacc("TRN2", target_bir_lowering=False, num_devices=1, dynamic_dma_scratch_size=64)
    arrays, ins, outs = {}, {}, {}
    for name, x in inputs.items():
        x = np.ascontiguousarray(x)
        arrays["in_" + name] = x
        ins[name] = nc.dram_tensor("in_" + name, x.shape, mybir.dt.from_np(x.dtype), kind="ExternalInput").ap()
    for name, shape in _OUTS:
        outs[name] = nc.dram_tensor("out_" + name, shape, F32, kind="ExternalOutput").ap()
    trunk(nc, ins, outs)
    r = run_bass_kernel_spmd(nc, [arrays], core_ids=[0])
    return tuple(r.results[0]["out_" + name] for name, _ in _OUTS)
```

```python
from contextlib import ExitStack

import numpy as np

import concourse.bass as bass
from concourse import mybir

F32 = mybir.dt.float32
F32R = mybir.dt.float32r
I32 = mybir.dt.int32
ALU = mybir.AluOpType
ACT = mybir.ActivationFunctionType

P = 128
D = 1024
KC = D // P
SEQ = 1024
META = 16
NPR = SEQ + META
DB, DQ = 8, 4
NS = DB * DQ
TOK = NPR + NS
G = 3
GW = 358
T = G * GW
NH, HD = 16, 64
PAST, PAGE = 256, 128
NPAGE = PAST // PAGE
CW = 3
NT = 9
LAST = TOK - 128 * (NT - 1)
LASTP = NPR - 128 * (NT - 1)
FF_BLK = 4
EPS = 1e-6
SCALE = HD ** -0.5
MASKED = -1e30 / SCALE

U_IN = 0
U_OUT = U_IN + 3 * KC
U_MLP = [U_OUT + KC, 0]
U_K = U_MLP[0] + 2 * KC * FF_BLK
U_V = U_K + KC
U_Q = U_V + KC
U_O = U_Q + KC
U_MLP[1] = U_O + KC
N_UNITS = U_MLP[1] + 2 * KC * FF_BLK

G_MIX = [0, KC]
G_MLP = [2 * KC, 3 * KC]
G_KV = 4 * KC
G_CONV = 5 * KC
G_KN = G_CONV + CW * KC
G_QN = G_KN + 1
N_VEC = G_QN + 1

SPLITS = [G_MIX[0], G_MLP[0], G_KV, G_MIX[1], G_MLP[1]]

AX_IN = 0
AX_VEC = AX_IN + 2 * NT
AX_ST = [0, 0, 0, 0]
AX_ST[0] = AX_VEC + 2
AX_CONV = AX_ST[0] + G
AX_ST[1] = AX_CONV + 2
AX_ST[2] = AX_ST[1] + G
AX_F = AX_ST[2] + G
AX_K = AX_F + G
AX_V = AX_K + 6 * KC
AX_LF = AX_V + 3 * KC
AX_Q = AX_LF + 1
AX_ST[3] = AX_Q + 3 * KC
AX_Y = AX_ST[3] + G

STEPS = 2 * NT
ORDER = [0, 7, 1, 6, 2, 5, 3, 4, 8]
BLOCKS = [min(t + 1, NT) for t in range(NT)]
GROUPS = [[range(4 * g, min(4 * g + 4, b)) for g in range(-(-b // 4))] if t < NT - 1 else [range(b)]
          for t, b in enumerate(BLOCKS)]
TURNS = [range(0, 3), range(3, 5), range(5, 7), range(7, 9)]
RING_P, RING_S, RING_O = {}, {}, []
RING = 0
for _n in range(STEPS):
    if ORDER[(_n + 2) % NT] == NT - 1:
        RING_S[(_n + 2) % STEPS] = RING
        RING += 1
    RING_P[_n] = RING
    RING += len(GROUPS[ORDER[_n % NT]])
    if _n == 1:
        RING_O = RING
        RING += len(TURNS)
N_GROUPS = 2 * sum(len(g) for g in GROUPS)
KEYS = PAST + NS


def trunk(nc, a, out):
    ctx = ExitStack()
    with ctx:
        at = [nc.sbuf_base + (-nc.sbuf_base) % 32]

        def place(name, shape, dt=F32, offset=None):
            size = 4 * int(np.prod(shape[1:]))
            size += -size % 32
            if offset is None:
                offset = at[0]
                at[0] += size
            return nc.alloc_sbuf_tensor_at(name, shape, dt, offset=offset), offset + size

        ACC, _ = place("acc", [P, KC, T])
        hid0 = at[0]
        HH, hid1 = place("hid_hi", [P, KC, T], F32R)
        HL, _ = place("hid_lo", [P, KC, T], F32R)
        KS, _ = place("k_all", [P, KC, T], offset=hid0)
        QS, _ = place("q_all", [P, KC, T], offset=hid1)
        IN, _ = place("tokens_in", [P, NT, D], offset=hid0)
        RAW, _ = place("w_raw", [P, 2, KC, P])
        WH, _ = place("w_hi", [P, 2, KC, P], F32R)
        WL, _ = place("w_lo", [P, 2, KC, P], F32R)
        ident, _ = place("ident", [P, P])
        ones, _ = place("ones", [P, P], F32R)
        heads1, _ = place("ones_per_head", [P, P], F32R)
        vecs, _ = place("vectors", [P, N_VEC])
        epst, _ = place("eps", [P, 1])
        lf0 = at[0]
        LF, _ = place("gate_logits", [NH, T])
        CST, cst1 = place("conv_states", [P, KC, DB * (CW - 1)], offset=lf0)
        UL, _ = place("conv_last", [P, KC, (DB + 1) * (CW - 1)], offset=cst1)
        VIN, _ = place("vectors_in", [N_VEC, P], offset=lf0 + 1088)
        att0 = at[0]
        XH, _ = place("x_hi", [P, KC, T], F32R)
        XL, _ = place("x_lo", [P, KC, T], F32R)
        R, _ = place("rms_inv", [P, T])
        t10 = at[0]
        T1, t1e = place("t1", [P, T])
        t20 = at[0]
        T2, _ = place("t2", [P, T + 16])
        T1R, _ = place("t1_r", [P, T], F32R, offset=t10)
        T2R, _ = place("t2_r", [P, T], F32R, offset=t20)
        kw0 = at[0]
        KW, kwe = place("k_work", [P, 2, T])
        ot0 = at[0]
        OT, _ = place("out_tiles", [P, NT, P])
        att1 = at[0]
        SQ = {}
        for half, offset in ((U_K, hid1), (U_Q, ot0)):
            odd, _ = place(f"squares{half}", [P, T], offset=offset)
            odd_r, _ = place(f"squares{half}_r", [P, T], F32R, offset=offset)
            SQ[half] = ((T1, T1R), (odd, odd_r))
        assert att1 <= nc.sbuf_usable_end - 24, att1
        STI, _ = place("states_in", [DB * (CW - 1), D], offset=kw0)
        CO, _ = place("conv_out", [(DB + 1) * (CW - 1), D], offset=kw0)
        YO, _ = place("y_out", [P, NT, D], offset=att0)
        WFR, o = place("wf_raw", [P, KC, NH], offset=kwe)
        WFH, o = place("wf_hi", [P, KC, NH], F32R, offset=o)
        WFL, o = place("wf_lo", [P, KC, NH], F32R, offset=o)
        BF, _ = place("b_f", [NH, 1], offset=att1)
        PTAB, o = place("page_ids", [1, DB * NPAGE], I32, offset=att1 + 32)
        assert o <= nc.sbuf_usable_end
        slot = 4 * T + (-4 * T) % 32
        Z, ZN, ZE, ZU = (place(n, [NH, T], offset=hid1 + slot * m)[0]
                         for m, n in enumerate(("gate_z", "gate_neg", "gate_exp", "gate_exp1")))
        LT, _ = place("logf_tiles", [P, NT, NH], offset=hid1 + slot * 5)
        C8, _ = place("minus_8_sums", [NH, NPR], offset=hid1 + slot * 6)
        c_rows = nc.dram_tensor("c_rows", [NH, NPR], F32, kind="Internal").ap()

        def areas(start):
            where = [start]

            def put(name, shape, dt=F32):
                t, where[0] = place(name, shape, dt, offset=where[0])
                assert where[0] <= att1, (name, where[0] - att1)
                return t
            return put, where

        put, prompt_end = areas(att0)
        QP = put("q_split", [P, 2, NPR], F32R)
        KP = put("k_twice", [P, 2, NPR], F32R)
        KL = put("k_lo", [P, NPR], F32R)
        NEGC = put("minus_8_c", [P, 2, NPR])
        VRAW = put("v_raw", [P, NT, P])
        LPG, _ = place("logf_page", [P, DB * NPAGE, NH],
                       offset=prompt_end[0] - 4 * DB * NPAGE * NH)
        VV = put("v_split", [P, 2, NT, 2, HD], F32R)
        PR = put("probs", [P, 3, NPR])
        PTH = put("probs_t_hi", [P, 2, SEQ], F32R)
        PTL = put("probs_t_lo", [P, 2, SEQ], F32R)
        OS = put("o_tiles", [P, NT, 2, HD])
        OP = put("o_part", [P, 2, HD])
        MASK = put("mask", [P, P], F32R)
        IDR = put("ident_r", [P, P], F32R)
        NEGM, RSUM, RINV = (put(n, [P, 8]) for n in ("minus_max", "row_sum", "row_inv"))
        MASKF, _ = place("mask_f32", [P, P], offset=prompt_end[0])
        put, _ = areas(prompt_end[0])
        KPG = put("k_page", [P, 2, NPAGE, D])
        VPH, o = place("v_page_hi", [P, 2, NPAGE, D], F32R, offset=hid0)
        VPL, o = place("v_page_lo", [P, 2, NPAGE, D], F32R, offset=o)
        assert o <= hid1
        put, decode_end = areas(att0)
        VPG = put("v_page", [P, 2, NPAGE, D])
        VDH = put("v_new_hi", [NS, D], F32R)
        VDL = put("v_new_lo", [NS, D], F32R)
        QBW = (NH * DQ + 2 * DQ) * KC + 2 * DQ
        QBH = put("q_blocks_hi", [P, QBW], F32R)
        QBL = put("q_blocks_lo", [P, QBW], F32R)
        HQ = NH * DQ
        DPH = put("d_probs_t_hi", [P, NPAGE + 1, HQ], F32R)
        DPL = put("d_probs_t_lo", [P, NPAGE + 1, HQ], F32R)
        SD = put("d_probs", [HQ, 2, KEYS])
        KTH = put("k_t_hi", [P, KC, KEYS], F32R)
        KTL = put("k_t_lo", [P, KC, KEYS], F32R)
        CSF = put("past_sums", [NH, PAST + DB * (KEYS + DQ)])
        CSH = put("sums_hi", [NH, KEYS], F32R)
        CSL = put("sums_lo", [NH, KEYS], F32R)
        OD = put("d_out", [HQ, D])
        EXF = put("expand_f32", [NH, HQ])
        EX = put("expand", [NH, HQ], F32R)
        MW = put("mask_wide", [HQ, NH, DQ])
        M4 = put("mask_new", [HQ, DQ])
        MB = put("mask_by_seq", [HQ, DB, NS])
        MBC = put("mask_row", [HQ, 2, KEYS])
        DST = put("d_stats", [HQ, 3, 2])
        assert decode_end[0] <= prompt_end[0]
        CS = CSF[:, 0:DB * KEYS].rearrange("h (b k) -> h b k", b=DB)
        CS_NEW = CSF[:, PAST:PAST + DB * (KEYS + DQ)].rearrange("h (b k) -> h b k", b=DB)[:, :, 0:DQ]
        UP = T2[:, 0:CW - 1 + NPR]
        US = T2[:, CW - 1 + NPR:CW - 1 + NPR + DB * (DQ + CW - 1)].rearrange("p (b t) -> p b t", b=DB)
        PS = ctx.enter_context(nc.psum_tensor("ps", [P, 8, 512], F32))

        def banks(x):
            return x.rearrange("p (g w) -> p g w", g=G)

        def sem(name):
            return ctx.enter_context(nc.semaphore(name))

        in_loaded = [sem(f"in_loaded{t}") for t in range(NT)]
        vec_loaded, state_loaded, gate_w_loaded = sem("vec_loaded"), sem("state_loaded"), sem("gate_w_loaded")
        w_loaded = [sem("w_loaded0"), sem("w_loaded1")]
        w_hi, w_lo = sem("w_hi"), sem("w_lo")
        unit_done, unit_read = sem("unit_done"), sem("unit_read")
        aux_done, aux_read = sem("aux_done"), sem("aux_read")
        const_ready, zero_ready, heads_zero = sem("const_ready"), sem("zero_ready"), sem("heads_zero")
        x_hi, x_lo, x_sq, x_ssq = sem("x_hi"), sem("x_lo"), sem("x_sq"), sem("x_ssq")
        ssq_hi, ssq_lo, rms_ready = sem("ssq_hi"), sem("ssq_lo"), sem("rms_ready")
        h_raw, hid_hi, hid_lo = sem("h_raw"), sem("hid_hi"), sem("hid_lo")
        u_ready, u_last, conv_step = sem("u_ready"), sem("u_last"), sem("conv_step")
        conv_stored = sem("conv_stored")
        z_sq, z_hi, z_lo, z_inv, z_fin = sem("z_sq"), sem("z_hi"), sem("z_lo"), sem("z_inv"), sem("z_fin")
        k_kept, kv_stored = sem("k_kept"), sem("kv_stored")
        gate_hi, gate_lo = sem("gate_hi"), sem("gate_lo")
        bf_loaded, gate_step, gate_act = sem("bf_loaded"), sem("gate_step"), sem("gate_act")
        logf_stored, c_stored = sem("logf_stored"), sem("c_stored")
        lt_kept = sem("lt_kept")
        p_const, p_round, v_zero = sem("p_const"), sem("p_round"), sem("v_zero")
        q_hi, q_lo, k_hi, k_dup, k_lo = sem("q_hi"), sem("q_lo"), sem("k_hi"), sem("k_dup"), sem("k_lo")
        v_loaded, v_hi, v_lo = sem("v_loaded"), sem("v_hi"), sem("v_lo")
        c_loaded = [sem("c_loaded0"), sem("c_loaded1")]
        s_done, s_used, e_done = sem("s_done"), sem("s_used"), sem("e_done")
        ring_done, ring_free, pt_hi = sem("ring_done"), sem("ring_free"), sem("pt_hi")
        pv_done, inv_ready, o_part, o_out = sem("pv_done"), sem("inv_ready"), sem("o_part"), sem("o_out")
        ids_loaded, lp_loaded, vn_loaded = sem("ids_loaded"), sem("lp_loaded"), sem("vn_loaded")
        dk_loaded, dv_loaded = ([sem(f"d{x}_loaded{i}") for i in range(2)] for x in "kv")
        d_const, d_mask, d_sums, new_hi, new_lo = (sem("d_const"), sem("d_mask"), sem("d_sums"),
                                                   sem("new_hi"), sem("new_lo"))
        past_done, past_kept, mb_ready = sem("past_done"), sem("past_kept"), sem("mb_ready")
        dt_done, dt_hi, dt_used = sem("dt_done"), sem("dt_hi"), sem("dt_used")
        qc_hi, qc_lo, dv_hi, dv_lo = sem("qc_hi"), sem("qc_lo"), sem("dv_hi"), sem("dv_lo")
        ds_done, ds_used, de_done, dn_done = sem("ds_done"), sem("ds_used"), sem("de_done"), sem("dn_done")
        dp_done, dp_hi, dp_used = sem("dp_done"), sem("dp_hi"), sem("dp_used")
        dw_done, dw_kept, do_done, do_used = sem("dw_done"), sem("dw_kept"), sem("do_done"), sem("do_used")
        o_hi, o_lo = sem("o_hi"), sem("o_lo")
        y_stored = sem("y_stored")

        def ge(eng, s, value):
            if not isinstance(value, (int, np.integer)) or value > 0:
                eng.wait_ge(s, value)

        wait_value = {}

        def ge_apart(eng, s, value):
            if not isinstance(value, (int, np.integer)):
                if eng not in wait_value:
                    wait_value[eng] = eng.alloc_register("wait_value")
                eng.reg_add(wait_value[eng], value, 0)
                eng.wait_ge(const_ready, 1)
                eng.wait_ge(s, wait_value[eng])
            else:
                ge(eng, s, value)

        def sides(t):
            return 128 * t, min(128, TOK - 128 * t)

        pe, act, dve, pool, sp = nc.tensor, nc.scalar, nc.vector, nc.gpsimd, nc.sync

        def load_unit(w, row0, col0, c, i=0, stride=2):
            u = c + stride * i
            ge_apart(sp, w_lo, u - 1)
            src = w.rearrange("(k p) n -> p k n", p=P)[:, row0:row0 + KC, bass.ds(col0, P)] \
                if isinstance(row0, int) else \
                w.rearrange("(k p) n -> p k n", p=P)[:, bass.ds(row0, KC), bass.ds(col0, P)]
            sp.dma_start(RAW[:, c % 2], src).then_inc(w_loaded[c % 2], 16)

        def round_unit(c, i=0, stride=2):
            if isinstance(i, int) and c + stride * i >= N_UNITS:
                return
            u, s = c + stride * i, c % 2
            act.wait_ge(w_loaded[s], 16 * (c // 2 + 1) + (16 * stride // 2) * i)
            ge(act, unit_done, u - 1)
            act.activation(WH[:, s], RAW[:, s], ACT.Copy).then_inc(w_hi, 1)

        def cut_unit(c, i=0, stride=2):
            if isinstance(i, int) and c + stride * i >= N_UNITS:
                return
            u, s = c + stride * i, c % 2
            dve.wait_ge(w_hi, u + 1)
            dve.tensor_tensor(WL[:, s], RAW[:, s], WH[:, s].bitcast(F32), ALU.subtract).then_inc(w_lo, 1)

        def unit(c, i=0, stride=2, hi=XH, lo=XL, ready=None, mid=None):
            u, s = c + stride * i, c % 2
            pe.wait_ge(w_lo, u + 1)
            ge(pe, unit_read, u - 1)
            for k in range(KC):
                if mid and k in mid:
                    mid[k]()
                if ready:
                    ready(k)
                for n, (w, x) in enumerate(((WH, hi), (WH, lo), (WL, hi))):
                    for g in range(G):
                        mm = pe.matmul(PS[:, G * s + g, 0:GW], w[:, s, k], x[:, k, g * GW:(g + 1) * GW],
                                       start=(k == 0 and n == 0), stop=(k == KC - 1 and n == 2))
            mm.then_inc(unit_done, 1)

        def result(c):
            return PS[:, G * (c % 2):G * (c % 2) + G, 0:GW]

        def residual_hi(split, m, square=None):
            act.activation(XH[:, m], ACC[:, m], ACT.Copy,
                           scale=vecs[:, bass.ds(SPLITS[split] + m, 1)]).then_inc(x_hi, 1)
            if square is None:
                return
            if isinstance(m, int) and m == 0:
                act.activation(T2[:, 0:T], ACC[:, m], ACT.Square).then_inc(x_ssq, 1)
            else:
                before = m - 1 if square == 0 else m
                ge_apart(act, x_ssq, 8 * square + before)
                act.activation(squares(square, m), ACC[:, m], ACT.Square).then_inc(x_sq, 1)

        def squares(f, m):
            return KW[:, 0] if f == 0 and m % 2 == 0 else T1[:, :]

        def residual_lo(split, m):
            dve.wait_ge(x_hi, 8 * split + m + 1)
            dve.scalar_tensor_tensor(XL[:, m], ACC[:, m], vecs[:, bass.ds(SPLITS[split] + m, 1)],
                                     XH[:, m].bitcast(F32), ALU.mult, ALU.subtract).then_inc(x_lo, 1)

        def residual_sum(f, m):
            pool.wait_ge(x_sq, (KC - 1) * f + m)
            pool.wait_ge(x_ssq, 8 * f + m)
            pool.tensor_tensor(T2[:, 0:T], T2[:, 0:T], squares(f, m), ALU.add).then_inc(x_ssq, 1)

        def rms_split_hi(s):
            act.wait_ge(x_ssq, 8 * (s + 1))
            act.activation(T1R[:, :], T2[:, 0:T], ACT.Copy).then_inc(ssq_hi, 1)

        def rms_split_lo(s):
            dve.wait_ge(ssq_hi, s + 1)
            dve.tensor_tensor(T2R[:, :], T2[:, 0:T], T1R[:, :].bitcast(F32), ALU.subtract).then_inc(ssq_lo, 1)

        def column_sums(first, weights, wait, hi=None, groups=range(G)):
            if 0 in groups:
                wait()
            for g in groups:
                b = 6 + (first + g) % 2 if isinstance(first, int) else 6 + (first[0] + g) % 2
                n = first if isinstance(first, int) else first[1]
                ge(pe, aux_read, n + g - 1)
                for x, stop in ((hi or T1R, False), (T2R, True)):
                    mm = pe.matmul(PS[:, b, 0:GW], weights[:, :], x[:, g * GW:(g + 1) * GW],
                                   start=not stop, stop=stop)
                mm.then_inc(aux_done, 1)

        def rms_root(s):
            for g in range(G):
                n = AX_ST[s] + g
                act.wait_ge(aux_done, n + 1)
                act.activation(R[:, g * GW:(g + 1) * GW], PS[:, 6 + n % 2, 0:GW], ACT.Sqrt,
                               scale=1.0 / D, bias=epst[:, 0:1]).then_inc(aux_read, 1)

        def rms_inverse(s):
            dve.wait_ge(aux_read, AX_ST[s] + G)
            dve.reciprocal(R[:, :], R[:, :]).then_inc(rms_ready, 1)
            dve.wait_ge(rms_ready, s + 1)

        def rms_sums(s):
            column_sums(AX_ST[s], ones, lambda: pe.wait_ge(ssq_lo, s + 1))

        def x_ready(split):
            return lambda k: pe.wait_ge(x_lo, 8 * split + k + 1)

        def turn_tokens(par, n, groups):
            for g in groups:
                pe_bank = 6 + (n[0] + g) % 2
                ge_apart(pe, aux_read, n[1] + g - 1)
                for t in range(4 * g, min(4 * g + 4, NT)):
                    tok, rows = sides(t)
                    mm = pe.transpose(PS[0:rows, pe_bank, P * (t % 4):P * (t % 4) + P],
                                      KW[:, par, tok:tok + rows], ident[:, :])
                mm.then_inc(aux_done, 1)

        def keep_tokens(n, stored):
            ge(act, kv_stored, 48 * stored)
            for g in range(G):
                act.wait_ge(aux_done, n[1] + g + 1)
                b = 6 + (n[0] + g) % 2
                if g < 2:
                    act.activation(OT[:, 4 * g:4 * g + 4, :].rearrange("p t c -> p (t c)"), PS[:, b, :],
                                   ACT.Copy).then_inc(aux_read, 1)
                else:
                    act.activation(OT[0:LAST, NT - 1, :], PS[0:LAST, b, 0:P], ACT.Copy).then_inc(aux_read, 1)

        def store_tokens(n, prompt, decode, m):
            act.wait_ge(aux_read, n[1] + G)
            full = P * (NT - 1)
            rows = prompt[0].rearrange("t h d -> t (h d)")
            act.dma_start(rows[0:full, bass.ds(P * m, P)].rearrange("(t p) c -> p t c", p=P),
                          OT[:, 0:NT - 1, :]).then_inc(kv_stored, 16)
            act.dma_start(rows[full:NPR, bass.ds(P * m, P)], OT[0:LASTP, NT - 1, :]).then_inc(kv_stored, 16)
            act.dma_start(decode.rearrange("b t h d -> (b t) (h d)")[:, bass.ds(P * m, P)],
                          OT[LASTP:LAST, NT - 1, :]).then_inc(kv_stored, 16)

        def ax(first, stride, i):
            return (first, first + stride * i)


        def halves(hh):
            return slice(HD * hh, HD * hh + HD), slice(HD - HD * hh, P - HD * hh)

        def step(n):
            hh, i = n // NT, ORDER[n % NT]
            return hh, i, (P if i < NT - 1 else LASTP)

        def ring(m, idx):
            if isinstance(m, int) and m == 0:
                return idx if idx < RING_O else idx - len(TURNS)
            return RING * m + idx - len(TURNS)

        def pt_index(m, n, g):
            return N_GROUPS * m + sum(len(GROUPS[ORDER[x % NT]]) for x in range(n)) + g

        def prep_act(m, hh, part):
            own, _ = halves(hh)
            if part == 0:
                ge_apart(act, s_done, STEPS * m + NT * hh - NT)
                act.activation(QP[own, hh], QS[own, m, 0:NPR], ACT.Copy).then_inc(q_hi, 1)
            elif part == 1:
                act.activation(KP[own, hh], KS[own, m, 0:NPR], ACT.Copy).then_inc(k_hi, 1)
            else:
                if hh == 0:
                    act.wait_ge(v_loaded, 32 * (m + 1))
                ge(act, pv_done, STEPS * m + NT * hh - NT)
                act.activation(VV[:, hh, :, 0], VRAW[:, :, HD * hh:HD * hh + HD], ACT.Copy)\
                   .then_inc(v_hi, 1)

        def prep_dve(m, hh, part):
            own, other = halves(hh)
            if part == 0:
                dve.wait_ge(q_hi, 2 * m + hh + 1)
                dve.tensor_tensor(QP[other, hh], QS[own, m, 0:NPR], QP[own, hh].bitcast(F32), ALU.subtract)\
                   .then_inc(q_lo, 1)
            else:
                dve.wait_ge(k_hi, 2 * m + hh + 1)
                dve.tensor_copy(KP[other, hh], KP[own, hh]).then_inc(k_dup, 1)

        def prep_pool(m, hh):
            own, _ = halves(hh)
            ge(pool, v_lo, 2 * m + hh)
            ge_apart(pool, k_hi, 2 * m + hh + 1)
            pool.tensor_tensor(KL[own, :], KS[own, m, 0:NPR], KP[own, hh].bitcast(F32), ALU.subtract)\
                .then_inc(k_lo, 1)
            pool.wait_ge(k_lo, 2 * m + hh + 1)
            pool.wait_ge(v_hi, 2 * m + hh + 1)
            pool.tensor_tensor(VV[:, hh, :, 1], VRAW[:, :, HD * hh:HD * hh + HD],
                               VV[:, hh, :, 0].bitcast(F32), ALU.subtract).then_inc(v_lo, 1)

        def logits(m, n):
            hh, i, rows = step(n % STEPS)
            if n >= STEPS:
                m, n = m + 1, n - STEPS
            s, b0 = STEPS * m + n, 2 * (n % 2)
            own, _ = halves(hh)
            if n % NT == 0:
                for ready in (q_lo, k_dup, k_lo):
                    pe.wait_ge(ready, 2 * m + hh + 1)
            ge(pe, s_used, s - 1)
            q = slice(P * i, P * i + rows)

            def part(out, cols, diagonal):
                mm = pe.matmul(out, QP[:, hh, q], KP[:, hh, cols], start=True, stop=False)
                mm = pe.matmul(out, QP[own, hh, q], KL[own, cols], start=False, stop=not diagonal)
                return mm

            wide = min(P * (i + 1), SEQ)
            for c0 in range(0, wide, 512):
                w = min(512, wide - c0)
                diagonal = i < NT - 1 and c0 + w == wide
                mm = part(PS[0:rows, b0 + c0 // 512, 0:w], slice(c0, c0 + w), diagonal)
                if diagonal:
                    mm = pe.matmul(PS[:, b0 + c0 // 512, w - P:w], IDR[:, :], MASK[:, :], start=False, stop=True)
            mm.then_inc(s_done, 1)
            if i == NT - 1:
                use, bank = ring(m, RING_S[n]), 4 + RING_S[n] % 2
                pe.wait_ge(ring_free, use - 1)
                out = PS[0:rows, bank, 0:LASTP]
                part(out, slice(SEQ, NPR), True)
                pe.matmul(out, IDR[0:rows, 0:rows], MASK[0:rows, 0:LASTP], start=False, stop=True)\
                  .then_inc(ring_done, 1)

        def max_logits(m, n):
            hh, i, rows = step(n % STEPS)
            if n >= STEPS:
                m, n = m + 1, n - STEPS
            s, b0, k = STEPS * m + n, 2 * (n % 2), n % 6
            if n % NT == 0:
                dve.wait_ge(c_loaded[hh], 16 * (m + 1))
            wide = min(P * (i + 1), SEQ)
            first = 3e38
            if i == NT - 1:
                use, bank = ring(m, RING_S[n]), 4 + RING_S[n] % 2
                ge_apart(dve, ring_done, use + 1)
                first = NEGM[0:rows, 6 + hh:7 + hh]
                dve.tensor_tensor_reduce(out=PR[0:rows, n % 3, SEQ:NPR], in0=PS[0:rows, bank, 0:LASTP],
                                         in1=NEGC[0:rows, hh, SEQ:NPR], scale=-SCALE, scalar=3e38,
                                         op0=ALU.add, op1=ALU.min, accum_out=first).then_inc(ring_free, 1)
                dve.wait_ge(ring_free, use + 1)
            ge_apart(dve, s_done, s + 1)
            dve.tensor_tensor_reduce(out=PR[0:rows, n % 3, 0:wide],
                                     in0=PS[0:rows, b0:b0 + 2, :].rearrange("p b w -> p (b w)")[:, 0:wide],
                                     in1=NEGC[0:rows, hh, 0:wide], scale=-SCALE, scalar=first,
                                     op0=ALU.add, op1=ALU.min, accum_out=NEGM[0:rows, k:k + 1])\
               .then_inc(s_used, 1)

        def exp_logits(m, n):
            hh, i, rows = step(n % STEPS)
            if n >= STEPS:
                m, n = m + 1, n - STEPS
            k, wide = n % 6, (P * (i + 1) if i < NT - 1 else NPR)
            act.wait_ge(s_used, STEPS * m + n + 1)
            x = PR[0:rows, n % 3, 0:wide]
            act.activation(x, x, ACT.Exp, scale=-1.0, bias=NEGM[0:rows, k:k + 1],
                           accum_out=RSUM[0:rows, k:k + 1]).then_inc(e_done, 1)

        def pt_groups(n):
            i = ORDER[n % NT]
            w = P if i < NT - 1 else LASTP
            return [(RING_P[n] + g, g, blocks, w) for g, blocks in enumerate(GROUPS[i])]

        def turn_probs(m, n):
            hh, i, rows = step(n)
            ge_apart(pe, e_done, STEPS * m + n + 1)
            for idx, g, blocks, w in pt_groups(n):
                ge_apart(pe, ring_free, ring(m, idx) - 1)
                for x, j in enumerate(blocks):
                    keys = min(P, NPR - P * j)
                    mm = pe.transpose(PS[0:keys, 4 + idx % 2, w * x:w * x + rows],
                                      PR[0:rows, n % 3, P * j:P * j + keys], ident[0:rows, 0:rows])
                mm.then_inc(ring_done, 1)

        def probs_hi(m, n):
            ge(act, pv_done, STEPS * m + n - 1)
            for idx, g, blocks, w in pt_groups(n):
                act.wait_ge(ring_done, ring(m, idx) + 1)
                a0, a1 = w * blocks[0], w * (blocks[-1] + 1)
                act.activation(PTH[:, n % 2, a0:a1], PS[:, 4 + idx % 2, 0:a1 - a0], ACT.Copy)\
                   .then_inc(pt_hi, 1)

        def probs_lo(m, n):
            for idx, g, blocks, w in pt_groups(n):
                dve.wait_ge(pt_hi, pt_index(m, n, g) + 1)
                a0, a1 = w * blocks[0], w * (blocks[-1] + 1)
                dve.tensor_tensor(PTL[:, n % 2, a0:a1], PS[:, 4 + idx % 2, 0:a1 - a0],
                                  PTH[:, n % 2, a0:a1].bitcast(F32), ALU.subtract).then_inc(ring_free, 1)

        def inverse_sums(m, n):
            rows, k = step(n)[2], n % 6
            dve.wait_ge(e_done, STEPS * m + n + 1)
            dve.reciprocal(RINV[0:rows, k:k + 1], RSUM[0:rows, k:k + 1]).then_inc(inv_ready, 1)

        def weigh_values(m, n):
            hh, i, rows = step(n)
            s, w = STEPS * m + n, (P if i < NT - 1 else LASTP)
            idx = pt_groups(n)[-1][0]
            if n % NT == 0:
                pe.wait_ge(v_lo, 2 * m + hh + 1)
            pe.wait_ge(ring_free, ring(m, idx) + 1)
            ge(pe, o_out, s - 1)
            last = BLOCKS[i] - 1
            for j in range(BLOCKS[i]):
                keys = min(P, NPR - P * j)
                pe.matmul(PS[0:rows, 6 + n % 2, 0:P], PTH[0:keys, n % 2, w * j:w * j + rows],
                          VV[0:keys, hh, j].rearrange("p x d -> p (x d)"), start=(j == 0), stop=False)
                mm = pe.matmul(PS[0:rows, 6 + n % 2, 0:HD], PTL[0:keys, n % 2, w * j:w * j + rows],
                               VV[0:keys, hh, j, 0], start=False, stop=(j == last))
            mm.then_inc(pv_done, 1)

        def output_part(m, n):
            rows, k, s = step(n)[2], n % 6, STEPS * m + n
            act.wait_ge(inv_ready, s + 1)
            act.wait_ge(pv_done, s + 1)
            ge(act, o_out, s - 1)
            act.activation(OP[0:rows, n % 2], PS[0:rows, 6 + n % 2, HD:P], ACT.Copy,
                           scale=RINV[0:rows, k:k + 1]).then_inc(o_part, 1)

        def output_tile(m, n):
            hh, i, rows = step(n)
            k = n % 6
            dve.wait_ge(o_part, STEPS * m + n + 1)
            dve.scalar_tensor_tensor(OS[0:rows, i, hh], PS[0:rows, 6 + n % 2, 0:HD], RINV[0:rows, k:k + 1],
                                     OP[0:rows, n % 2], ALU.mult, ALU.add).then_inc(o_out, 1)

        def turn_output(m):
            pe.wait_ge(o_out, STEPS * m)
            for g, tiles in enumerate(TURNS):
                idx = RING_O + g
                pe.wait_ge(ring_free, RING * m + idx - len(TURNS) - 1 - (RING_O if isinstance(m, int) and m == KC else 0))
                for x, t in enumerate(tiles):
                    rows = min(P, NPR - P * t)
                    mm = pe.transpose(PS[:, 4 + idx % 2, P * x:P * x + rows],
                                      OS[0:rows, t].rearrange("p h d -> p (h d)"), ident[0:rows, 0:rows])
                mm.then_inc(ring_done, 1)

        def keep_output(m):
            for g, tiles in enumerate(TURNS):
                idx = RING_O + g
                dve.wait_ge(ring_done, RING * m + idx - len(TURNS) + 1
                            - (RING_O if isinstance(m, int) and m == KC else 0))
                t0, t1 = P * tiles[0], min(P * (tiles[-1] + 1), NPR)
                dve.tensor_copy(QS[:, m - 1, t0:t1], PS[:, 4 + idx % 2, 0:t1 - t0]).then_inc(ring_free, 1)

        PROMPT_GROUPS = RING * KC

        def d_turn_keys(i, c, x):
            if x == 0:
                pe.wait_ge(dk_loaded[c], 32 * (i + 1))
            g, h = x // 2, x % 2
            ge(pe, dt_used, 4 * (c + 2 * i) + x - 1)
            for k in range(4):
                f = P * (4 * h + k)
                mm = pe.transpose(PS[:, x % 2, P * k:P * k + P], KPG[:, c, g, f:f + P], ident[:, :])
            mm.then_inc(dt_done, 1)

        def d_groups():
            return [(2 * g + h, (slice(None), slice(4 * h, 4 * h + 4), slice(PAGE * g, PAGE * g + PAGE)))
                    for g in range(NPAGE) for h in range(2)]

        def ps_turned(x):
            return PS[:, x % 2, :].rearrange("p (k t) -> p k t", k=4)

        def q_blocks(t, hh):
            w = NH * DQ + 2 * DQ
            return t[HD * hh:HD * hh + HD, DQ * hh:DQ * hh + w * KC].rearrange("p (m x) -> p m x", x=w)[:, :, 0:DQ]

        def d_hi(i, c):
            b = c + 2 * i
            ge(act, ds_done, b)
            for x, to in d_groups():
                act.wait_ge(dt_done, 4 * b + x + 1)
                act.activation(KTH[to], ps_turned(x), ACT.Copy).then_inc(dt_hi, 1)
            for hh in range(2):
                act.activation(q_blocks(QBH, hh), QS[HD * hh:HD * hh + HD, :, bass.ds(NPR + DQ * b, DQ)],
                               ACT.Copy).then_inc(qc_hi, 1)
            act.activation(CSH[:, :], CS[:, b], ACT.Copy, scale=-1.0 / SCALE).then_inc(qc_hi, 1)

        def d_lo(i, c):
            b = c + 2 * i
            for x, to in d_groups():
                dve.wait_ge(dt_hi, 4 * b + x + 1)
                dve.tensor_tensor(KTL[to], ps_turned(x), KTH[to].bitcast(F32), ALU.subtract).then_inc(dt_used, 1)
            dve.wait_ge(qc_hi, 3 * (b + 1))
            for hh in range(2):
                dve.tensor_tensor(q_blocks(QBL, hh), QS[HD * hh:HD * hh + HD, :, bass.ds(NPR + DQ * b, DQ)],
                                  q_blocks(QBH, hh).bitcast(F32), ALU.subtract).then_inc(qc_lo, 1)
            dve.scalar_tensor_tensor(CSL[:, :], CS[:, b], -1.0 / SCALE, CSH[:, :].bitcast(F32),
                                     ALU.mult, ALU.subtract).then_inc(qc_lo, 1)

        def d_logits(i, c):
            b = c + 2 * i
            pe.wait_ge(dt_used, 4 * (b + 1))
            pe.wait_ge(qc_lo, 3 * (b + 1))
            ge(pe, ds_used, b - 1)
            out = PS[0:HQ, 2 + c, 0:KEYS]
            for m in range(KC):
                for q, k in ((QBH, KTH), (QBH, KTL), (QBL, KTH)):
                    pe.matmul(out, q[:, HQ * m:HQ * m + HQ], k[:, m], start=(m == 0 and q is QBH and k is KTH),
                              stop=False)
            pe.matmul(out, EX[:, :], CSH[:, :], start=False, stop=False)
            pe.matmul(out, EX[:, :], CSL[:, :], start=False, stop=True).then_inc(ds_done, 1)

        def d_max(i, c):
            b = c + 2 * i
            ge_apart(dve, ds_done, b + 1)
            ge_apart(dve, mb_ready, b + 1)
            dve.tensor_tensor_reduce(out=SD[:, c], in0=PS[0:HQ, 2 + c, 0:KEYS], in1=MBC[:, c], scale=-SCALE,
                                     scalar=3e38, op0=ALU.add, op1=ALU.min, accum_out=DST[:, 0, c:c + 1])\
               .then_inc(ds_used, 1)

        def d_exp(i, c):
            act.wait_ge(ds_used, c + 2 * i + 1)
            act.activation(SD[:, c], SD[:, c], ACT.Exp, scale=-1.0, bias=DST[:, 0, c:c + 1],
                           accum_out=DST[:, 1, c:c + 1]).then_inc(de_done, 1)

        def d_norm(i, c):
            b = c + 2 * i
            dve.wait_ge(de_done, b + 1)
            dve.reciprocal(DST[:, 2, c:c + 1], DST[:, 1, c:c + 1]).then_inc(dn_done, 1)
            dve.wait_ge(dn_done, 2 * b + 1)
            dve.tensor_scalar(SD[:, c], SD[:, c], DST[:, 2, c:c + 1], None, ALU.mult).then_inc(dn_done, 1)

        def d_turn_probs(i, c):
            b = c + 2 * i
            ge_apart(pe, do_used, 4 * (b - 1))
            ge_apart(pe, dn_done, 2 * b + 2)
            for g in range(NPAGE + 1):
                keys = min(P, KEYS - P * g)
                mm = pe.transpose(PS[0:keys, 4 + c, HQ * g:HQ * g + HQ], SD[:, c, P * g:P * g + keys],
                                  ident[0:HQ, 0:HQ])
            mm.then_inc(dp_done, 1)

        def d_probs_hi(i, c):
            b = c + 2 * i
            act.wait_ge(dp_done, b + 1)
            ge(act, dw_done, 2 * b)
            act.activation(DPH[:, :, :].rearrange("p g r -> p (g r)"), PS[:, 4 + c, 0:(NPAGE + 1) * HQ],
                           ACT.Copy).then_inc(dp_hi, 1)

        def d_probs_lo(i, c):
            b = c + 2 * i
            dve.wait_ge(dp_hi, b + 1)
            dve.tensor_tensor(DPL[:, :, :].rearrange("p g r -> p (g r)"), PS[:, 4 + c, 0:(NPAGE + 1) * HQ],
                              DPH[:, :, :].rearrange("p g r -> p (g r)").bitcast(F32), ALU.subtract)\
               .then_inc(dp_used, 1)

        def d_values_hi(i, c):
            b = c + 2 * i
            act.wait_ge(dv_loaded[c], 32 * (i + 1))
            ge(act, dw_done, 2 * b - 2)
            act.activation(VPH[:, c], VPG[:, c], ACT.Copy).then_inc(dv_hi, 1)

        def d_values_lo(i, c):
            dve.wait_ge(dv_hi, c + 2 * i + 1)
            dve.tensor_tensor(VPL[:, c], VPG[:, c], VPH[:, c].bitcast(F32), ALU.subtract)\
               .then_inc(dv_lo, 1)

        def d_weigh(i, c, turn=None):
            b = c + 2 * i
            pe.wait_ge(dv_lo, b + 1)
            pe.wait_ge(dp_used, b + 1)
            ge(pe, dw_kept, 2 * b)
            for h in range(2):
                f = slice(512 * h, 512 * h + 512)
                for g in range(NPAGE + 1):
                    for n in range(3):
                        pr = DPL if n == 1 else DPH
                        if g < NPAGE:
                            left, right = pr[:, g], (VPL if n == 2 else VPH)[:, c, g, f]
                        else:
                            left, right = pr[0:NS, g], (VDL if n == 2 else VDH)[:, f]
                        mm = pe.matmul(PS[0:HQ, 6 + h, :], left, right, start=(g == 0 and n == 0),
                                       stop=(g == NPAGE and n == 2))
                mm.then_inc(dw_done, 1)
            if turn:
                for x in range(4):
                    d_turn_keys(*turn, x)
            ge_apart(pe, dw_kept, 2 * b + 2)
            for m in range(KC):
                mm = pe.transpose(PS[:, 4 + c, HQ * m:HQ * m + HQ], OD[:, P * m:P * m + P], ident[0:HQ, 0:HQ])
            mm.then_inc(do_done, 1)

        def d_keep(i, c):
            b = c + 2 * i
            ge(act, do_done, b)
            for h in range(2):
                act.wait_ge(dw_done, 2 * b + h + 1)
                act.activation(OD[:, 512 * h:512 * h + 512], PS[0:HQ, 6 + h, :], ACT.Copy).then_inc(dw_kept, 1)

        def d_output(i, c):
            b = c + 2 * i
            ge_apart(act, do_done, b + 1)
            w = HQ + 2 * DQ
            for hh in range(2):
                half = slice(HD * hh, HD * hh + HD)
                for m0, m1 in ((0, KC - 1), (KC - 1, KC)):
                    src = PS[half, 4 + c, w * m0 + DQ * hh:w * (m1 - 1) + DQ * hh + DQ] if m1 - m0 == 1 else \
                        PS[half, 4 + c, DQ * hh:DQ * hh + w * (KC - 1)].rearrange("p (m x) -> p m x", x=w)[:, :, 0:DQ]
                    to = QS[half, m0, bass.ds(NPR + DQ * b, DQ)] if m1 - m0 == 1 else \
                        QS[half, m0:m1, bass.ds(NPR + DQ * b, DQ)]
                    act.activation(to, src, ACT.Copy).then_inc(do_used, 1)

        def attention_loads():
            vp = out["v_prompt"][0].rearrange("t h d -> t (h d)")
            full = P * (NT - 1)

            def load_v(m):
                ge_apart(sp, v_lo, 2 * m)
                sp.dma_start(VRAW[:, 0:NT - 1], vp[0:full, bass.ds(P * m, P)].rearrange("(t p) c -> p t c", p=P))\
                  .then_inc(v_loaded, 16)
                sp.dma_start(VRAW[0:LASTP, NT - 1], vp[full:NPR, bass.ds(P * m, P)]).then_inc(v_loaded, 16)

            def load_c(m, hh):
                ge_apart(sp, s_used, STEPS * m + NT * hh - NT)
                sp.dma_start(NEGC[:, hh], c_rows[bass.ds(2 * m + hh, 1)].to_broadcast([P, NPR]))\
                  .then_inc(c_loaded[hh], 16)

            sp.wait_ge(unit_done, U_O)
            sp.wait_ge(z_fin, 2 * KC)
            sp.wait_ge(kv_stored, 48 * 2 * KC)
            sp.wait_ge(c_stored, 16)
            sp.wait_ge(v_zero, 1)
            load_v(0)
            load_c(0, 0)
            def pair(m):
                load_c(m, 1)
                load_v(m + 1)
                load_c(m + 1, 0)
            pair(0)
            with sp.Fori(1, KC - 1) as m:
                pair(m)
            load_c(KC - 1, 1)

            sp.wait_ge(ids_loaded, 16)

            def load_pages(cache, to, index, done):
                for g in range(NPAGE):
                    page = sp.value_load(PTAB[0:1, bass.ds(index + g, 1)], min_val=0,
                                         max_val=a["cache_k"].shape[0] - 1)
                    sp.dma_start(to[:, g], cache[bass.ds(page, 1)].rearrange("o t h d -> (o t) (h d)"))\
                      .then_inc(done, 16)

            def load_k(i, c):
                load_pages(a["cache_k"], KPG[:, c], NPAGE * (c + 2 * i), dk_loaded[c])

            sp.wait_ge(p_round, 2)
            load_k(0, 0)
            load_k(0, 1)
            sp.wait_ge(v_lo, 2 * KC)
            with sp.Fori(0, DB * NPAGE) as x:
                page = sp.value_load(PTAB[0:1, bass.ds(x, 1)], min_val=0, max_val=a["cache_k"].shape[0] - 1)
                sp.dma_start(LPG[:, x], a["cache_logf"][bass.ds(page, 1)].rearrange("o t h -> (o t) h"))\
                  .then_inc(lp_loaded, 16)
            sp.wait_ge(ring_free, PROMPT_GROUPS)
            sp.dma_start(VPG[0:NS, 1, 0], out["v_sample"].rearrange("b t h d -> (b t) (h d)"))\
              .then_inc(vn_loaded, 16)

            def load_v_pages(i, c):
                load_pages(a["cache_v"], VPG[:, c], NPAGE * (c + 2 * i), dv_loaded[c])
            load_v_pages(0, 0)
            sp.wait_ge(new_lo, 2)
            load_v_pages(0, 1)
            with sp.Fori(1, DB // 2) as i:
                for c in range(2):
                    ge_apart(sp, dt_done, 4 * (c + 2 * i - 1))
                    load_k(i, c)
                    ge_apart(sp, dv_lo, c + 2 * i - 1)
                    load_v_pages(i, c)

        def attention_pool():
            pool.wait_ge(unit_done, U_O)
            pool.wait_ge(z_fin, 2 * KC)
            pool.wait_ge(k_kept, KC)
            pool.memset(VRAW[:, NT - 1], 0.0).then_inc(v_zero, 1)
            pool.memset(MASKF[:, :], 0.0).then_inc(p_const, 1)
            pool.wait_ge(p_const, 1)
            pool.affine_select(out=MASKF[:, :], in_=MASKF[:, :], compare_op=ALU.is_ge, fill=MASKED, base=0,
                               pattern=[[-1, P]], channel_multiplier=1).then_inc(p_const, 1)
            prep_pool(0, 0)
            prep_pool(0, 1)
            with pool.Fori(1, KC) as m:
                prep_pool(m, 0)
                prep_pool(m, 1)

            pool.wait_ge(ring_free, PROMPT_GROUPS)
            for t, x in ((QBH[:, :].bitcast(F32), 0.0), (QBL[:, :].bitcast(F32), 0.0), (CSF[:, :], 0.0), (EXF[:, :], 1.0),
                         (MW[:, :, :], MASKED), (MB[:, :, :], MASKED), (MBC[:, :, :], 0.0)):
                pool.memset(t, x).then_inc(d_const, 1)
            pool.wait_ge(d_const, 7)
            pool.affine_select(out=EXF[:, :], in_=EXF[:, :], compare_op=ALU.is_ge, fill=0.0, base=0,
                               pattern=[[1, HQ]], channel_multiplier=-DQ).then_inc(d_const, 1)
            pool.affine_select(out=MW[:, :, :], in_=MW[:, :, :], compare_op=ALU.is_ge, fill=0.0, base=-1,
                               pattern=[[DQ, NH], [1, DQ]], channel_multiplier=-1).then_inc(d_const, 1)
            pool.wait_ge(d_const, 9)
            pool.affine_select(out=EXF[:, :], in_=EXF[:, :], compare_op=ALU.is_ge, fill=0.0, base=DQ - 1,
                               pattern=[[-1, HQ]], channel_multiplier=DQ).then_inc(d_const, 1)
            pool.affine_select(out=MW[:, :, :], in_=MW[:, :, :], compare_op=ALU.is_ge, fill=0.0, base=0,
                               pattern=[[-DQ, NH], [0, DQ]], channel_multiplier=1).then_inc(d_const, 1)
            pool.wait_ge(d_mask, DB + 1)

            def mask_of(i):
                for c in range(2):
                    b = c + 2 * i
                    ge_apart(pool, ds_used, b - 1)
                    pool.tensor_copy(MBC[:, c, PAST:KEYS], MB[:, b]).then_inc(mb_ready, 1)
            mask_of(0)
            with pool.Fori(1, DB // 2) as i:
                mask_of(i)

        def attention_scalar():
            act.wait_ge(unit_done, U_O)
            act.wait_ge(z_fin, 2 * KC)
            act.wait_ge(p_const, 2)
            act.activation(MASK[:, :], MASKF[:, :], ACT.Copy).then_inc(p_round, 1)
            act.activation(IDR[:, :], ident[:, :], ACT.Copy).then_inc(p_round, 1)
            prep_act(0, 0, 0)
            prep_act(0, 0, 1)
            prep_act(0, 0, 2)
            exp_logits(0, 0)

            def body(m, first=False, last=False):
                for n in range(STEPS):
                    probs_hi(m, n)
                    if not last or n + 1 < STEPS:
                        exp_logits(m, n + 1)
                    if n == 0 and not first:
                        output_part(m - 1, STEPS - 1)
                    if n > 0:
                        output_part(m, n - 1)
                    if n in (1, 2, 3):
                        prep_act(m, 1, n - 1)
                    if n in (10, 11, 12) and not last:
                        prep_act(m + 1, 0, n - 10)

            body(0, first=True)
            with act.Fori(1, KC - 1) as m:
                body(m)
            body(KC - 1, last=True)
            output_part(KC - 1, STEPS - 1)

            act.wait_ge(ring_free, PROMPT_GROUPS)
            act.activation(KTH[:, :, PAST:KEYS], KS[:, :, NPR:TOK], ACT.Copy).then_inc(new_hi, 1)
            act.wait_ge(vn_loaded, 16)
            act.activation(VDH[:, :], VPG[0:NS, 1, 0], ACT.Copy).then_inc(new_hi, 1)
            act.wait_ge(d_const, 11)
            act.activation(EX[:, :], EXF[:, :], ACT.Copy).then_inc(new_hi, 1)
            for g in range(4):
                act.wait_ge(past_done, g + 1)
                act.activation(CS[:, 2 * g:2 * g + 2, 0:PAST],
                               PS[0:NH, 4 + g % 2, :].rearrange("h (b k) -> h b k", b=2), ACT.Copy)\
                   .then_inc(past_kept, 1)
            act.activation(CS_NEW, LF[:, NPR:TOK].rearrange("h (b k) -> h b k", b=DB), ACT.Copy)\
               .then_inc(past_kept, 1)
            act.wait_ge(d_sums, DB)
            act.wait_ge(new_lo, 1)
            d_hi(0, 0)
            d_values_hi(0, 0)
            d_exp(0, 0)
            d_hi(0, 1)

            def pair(i, last=False):
                for c in range(2):
                    d_probs_hi(i, c)
                    if c == 0 or not last:
                        d_values_hi(i + c, 1 - c)
                        d_exp(i + c, 1 - c)
                    d_keep(i, c)
                    if not last:
                        d_hi(i + 1, c)
                    d_output(i, c)
            pair(0)
            with act.Fori(1, DB // 2 - 1) as i:
                pair(i)
            pair(DB // 2 - 1, True)

            act.wait_ge(do_used, 4 * DB)
            for m in range(KC):
                act.activation(HH[:, m], QS[:, m], ACT.Copy).then_inc(o_hi, 1)

        def attention_vector():
            dve.wait_ge(unit_done, U_O)
            dve.wait_ge(z_fin, 2 * KC)
            prep_dve(0, 0, 0)
            prep_dve(0, 0, 1)
            max_logits(0, 0)
            max_logits(0, 1)

            def body(m, first=False, last=False):
                for n in range(STEPS):
                    if not last or n + 2 < STEPS:
                        max_logits(m, n + 2)
                    probs_lo(m, n)
                    inverse_sums(m, n)
                    if n == 0 and not first:
                        output_tile(m - 1, STEPS - 1)
                    if n == 1 and not first:
                        keep_output(m)
                    if n > 0:
                        output_tile(m, n - 1)
                    if n in (3, 5):
                        prep_dve(m, 1, (n - 3) // 2)
                    if n in (12, 14) and not last:
                        prep_dve(m + 1, 0, (n - 12) // 2)

            body(0, first=True)
            with dve.Fori(1, KC - 1) as m:
                body(m)
            body(KC - 1, last=True)
            output_tile(KC - 1, STEPS - 1)
            keep_output(KC)

            dve.wait_ge(new_hi, 1)
            dve.tensor_tensor(KTL[:, :, PAST:KEYS], KS[:, :, NPR:TOK], KTH[:, :, PAST:KEYS].bitcast(F32),
                              ALU.subtract).then_inc(new_lo, 1)
            dve.wait_ge(new_hi, 2)
            dve.tensor_tensor(VDL[:, :], VPG[0:NS, 1, 0], VDH[:, :].bitcast(F32), ALU.subtract).then_inc(new_lo, 1)
            dve.wait_ge(d_const, 11)
            dve.tensor_reduce(M4[:, :], MW[:, :, :].rearrange("r h j -> r j h"), mybir.AxisListType.X, ALU.add)\
               .then_inc(d_mask, 1)
            dve.wait_ge(d_mask, 1)
            for b in range(DB):
                dve.tensor_copy(MB[:, b, DQ * b:DQ * b + DQ], M4[:, :]).then_inc(d_mask, 1)
            dve.wait_ge(past_kept, 5)
            for b in range(DB):
                dve.tensor_tensor_scan(CS[:, b], ones[0:NH, 0:1].bitcast(F32).to_broadcast([NH, KEYS]), CS[:, b],
                                       0.0, ALU.mult, ALU.add).then_inc(d_sums, 1)
            d_lo(0, 0)
            d_values_lo(0, 0)
            d_max(0, 0)
            d_norm(0, 0)
            d_lo(0, 1)

            def pair(i, last=False):
                for c in range(2):
                    d_probs_lo(i, c)
                    if c == 0 or not last:
                        d_max(i + c, 1 - c)
                        d_values_lo(i + c, 1 - c)
                        d_norm(i + c, 1 - c)
                    if not last:
                        d_lo(i + 1, c)
            pair(0)
            with dve.Fori(1, DB // 2 - 1) as i:
                pair(i)
            pair(DB // 2 - 1, True)
            for m in range(KC):
                dve.wait_ge(o_hi, m + 1)
                dve.tensor_tensor(HL[:, m], QS[:, m], HH[:, m].bitcast(F32), ALU.subtract).then_inc(o_lo, 1)

        def attention_tensor():
            pe.wait_ge(p_round, 2)
            logits(0, 0)
            logits(0, 1)

            def body(m, first=False, last=False):
                for n in range(STEPS):
                    if not last or n + 2 < STEPS:
                        logits(m, n + 2)
                    turn_probs(m, n)
                    if n == 1 and not first:
                        turn_output(m)
                    if n == 0 and not first:
                        weigh_values(m - 1, STEPS - 1)
                    if n > 0:
                        weigh_values(m, n - 1)

            body(0, first=True)
            with pe.Fori(1, KC - 1) as m:
                body(m)
            body(KC - 1, last=True)
            weigh_values(KC - 1, STEPS - 1)
            turn_output(KC)

            pe.wait_ge(lp_loaded, 16 * DB * NPAGE)
            pe.wait_ge(ring_free, PROMPT_GROUPS)
            for g in range(4):
                ge(pe, past_kept, g - 1)
                for x in range(4):
                    mm = pe.transpose(PS[0:NH, 4 + g % 2, P * x:P * x + P], LPG[:, 4 * g + x], ident[:, :])
                mm.then_inc(past_done, 1)
            pe.wait_ge(new_lo, 2)
            pe.wait_ge(new_hi, 3)
            for x in range(4):
                d_turn_keys(0, 0, x)
            d_logits(0, 0)
            for x in range(4):
                d_turn_keys(0, 1, x)

            def pair(i, last=False):
                for c in range(2):
                    if c == 0 or not last:
                        d_logits(i + c, 1 - c)
                    d_turn_probs(i, c)
                    d_weigh(i, c, None if last else (i + 1, c))
            pair(0)
            with pe.Fori(1, DB // 2 - 1) as i:
                pair(i)
            pair(DB // 2 - 1, True)

        def o_ready(k):
            pe.wait_ge(o_lo, k + 1)

        def turn_y(c, t):
            def f():
                tok, rows = sides(t)
                n = AX_Y + NT * c + t
                pe.wait_ge(aux_read, n - 1)
                if t == 0:
                    pe.wait_ge(unit_read, N_UNITS - 4 + 4 * c)
                for k in range(4):
                    mm = pe.transpose(PS[0:rows, 6 + n % 2, P * k:P * k + P], ACC[:, 4 * c + k, tok:tok + rows],
                                      ident[:, :])
                mm.then_inc(aux_done, 1)
            return f

        def y_tensor():
            unit(N_UNITS - 1, 0, 2, HH, HL, mid={k: turn_y(0, k) for k in range(KC)})
            turn_y(0, NT - 1)()
            for t in range(NT):
                turn_y(1, t)()

        def y_scalar():
            act.wait_ge(unit_done, U_MLP[1] + KC * (2 * FF_BLK - 1))
            for c in range(2):
                for t in range(NT):
                    rows, n = sides(t)[1], AX_Y + NT * c + t
                    act.wait_ge(aux_done, n + 1)
                    act.activation(YO[0:rows, t, 512 * c:512 * c + 512], PS[0:rows, 6 + n % 2, :], ACT.Copy)\
                       .then_inc(aux_read, 1)

        def y_vector():
            pass

        def store_y():
            y, ys = out["y_prompt"][0], out["y_sample"].rearrange("b t d -> (b t) d")
            for c in range(2):
                f = slice(512 * c, 512 * c + 512)
                for t in range(NT):
                    sp.wait_ge(aux_read, AX_Y + NT * c + t + 1)
                    if t == 0:
                        sp.dma_start(y[0:P - META, f], YO[META:P, 0, f]).then_inc(y_stored, 16)
                    elif t < NT - 1:
                        sp.dma_start(y[P * t - META:P * t - META + P, f], YO[:, t, f]).then_inc(y_stored, 16)
                    else:
                        sp.dma_start(y[SEQ - LASTP:SEQ, f], YO[0:LASTP, t, f]).then_inc(y_stored, 16)
                        sp.dma_start(ys[:, f], YO[LASTP:LAST, t, f]).then_inc(y_stored, 16)
            sp.wait_ge(y_stored, 2 * 16 * (NT + 1))
            sp.wait_ge(kv_stored, 48 * 2 * KC)
            sp.wait_ge(logf_stored, 48)
            sp.wait_ge(c_stored, 16)
            sp.wait_ge(conv_stored, 32)

        block = ctx.enter_context(nc.Block())

        MIX_COL = (1, 2, 0)
        HID = [KC, 2 * KC + FF_BLK * KC - KC]

        @block.sync
        def _(sync):
            xs = a["x_sample"].rearrange("b t d -> (b t) d")
            xp = a["x_prompt"][0]
            for g, x in ((G_MIX[0], a["norm_mix"].rearrange("l (k p) -> (l k) p", p=P)),
                         (G_MLP[0], a["norm_mlp"].rearrange("l (k p) -> (l k) p", p=P)),
                         (G_KV, a["norm_kv"].rearrange("(k p) -> k p", p=P)),
                         (G_CONV, a["conv_w"][0].rearrange("j (k p) -> (j k) p", p=P))):
                sp.dma_start(VIN[g:g + x.shape[0], :], x).then_inc(vec_loaded, 16)
            for g, x in ((G_KN, a["k_norm"].rearrange("(o d) -> o d", o=1)), (G_QN, a["q_norm"])):
                for half in range(2):
                    sp.dma_start(VIN[g:g + 1, half * HD:(half + 1) * HD], x).then_inc(vec_loaded, 16)
            sp.dma_start(STI[:, :], a["state_conv"][0].rearrange("b j d -> (b j) d")).then_inc(state_loaded, 16)
            sp.dma_start(IN[0:META, 0], a["meta_tokens"]).then_inc(in_loaded[0], 16)
            sp.dma_start(IN[META:P, 0], xp[0:P - META]).then_inc(in_loaded[0], 16)
            for t in range(1, NT - 1):
                sp.dma_start(IN[:, t], xp[P * t - META:P * t - META + P]).then_inc(in_loaded[t], 16)
            sp.dma_start(IN[0:LASTP, NT - 1], xp[SEQ - LASTP:SEQ]).then_inc(in_loaded[NT - 1], 16)
            sp.dma_start(IN[LASTP:LAST, NT - 1], xs).then_inc(in_loaded[NT - 1], 16)

            def mixer(i):
                for m2 in range(2):
                    for j in range(3):
                        load_unit(a["conv_w_in"][0], 0, MIX_COL[j] * D + P * m2 + 2 * P * i,
                                  3 * m2 + j, i, 6)

            def columns(u0, w, col0=0, row0=0, turn=0):
                with sp.Fori(0, KC // 2) as i:
                    for c in range(2):
                        load_unit(w, row0, col0 + P * c + 2 * P * i, u0 + c, turn + i)

            def mlp(l):
                with sp.Fori(0, FF_BLK) as b:
                    columns(U_MLP[l], a["mlp_w1"][l], D * b, 0, KC * b)
                    columns(U_MLP[l] + KC, a["mlp_w2"][l], 0, KC * b, KC * b)

            mixer(0)
            sp.dma_start(PTAB[:, :], a["page_table"].rearrange("b g -> (b g)").rearrange("(o n) -> o n", o=1))\
              .then_inc(ids_loaded, 16)
            sp.dma_start(BF[:, :], a["b_f"].rearrange("(n o) -> n o", o=1)).then_inc(bf_loaded, 16)
            sp.dma_start(WFR[:, :, :], a["w_f"].rearrange("(k p) n -> p k n", p=P)).then_inc(gate_w_loaded, 16)
            with sp.Fori(1, KC // 2) as i:
                mixer(i)
            columns(U_OUT, a["conv_w_out"][0])
            sp.wait_ge(aux_read, AX_CONV + 2)
            sp.dma_start(out["conv_prompt"][0, 0], CO[0:CW - 1, :]).then_inc(conv_stored, 16)
            sp.dma_start(out["conv_sample"][0].rearrange("b j d -> (b j) d"),
                         CO[CW - 1:(DB + 1) * (CW - 1), :]).then_inc(conv_stored, 16)
            mlp(0)
            columns(U_K, a["w_kv"])
            columns(U_V, a["w_kv"], D)
            columns(U_Q, a["w_q"][0])
            for c in range(2):
                load_unit(a["w_o"][0], 0, P * c, U_O + c)
            attention_loads()
            with sp.Fori(1, KC // 2) as i:
                for c in range(2):
                    load_unit(a["w_o"][0], 0, P * c + 2 * P * i, U_O + c, i)
            mlp(1)
            store_y()

        @block.gpsimd
        def _(gpsimd):
            pool.memset(ident[:, :], 0.0).then_inc(zero_ready, 1)
            pool.wait_ge(zero_ready, 1)
            pool.affine_select(out=ident[:, :], in_=ident[:, :], compare_op=ALU.not_equal, fill=1.0, base=0,
                               pattern=[[-1, P]], channel_multiplier=1).then_inc(const_ready, 1)
            pool.memset(ACC[:, :, TOK:T], 0.0).then_inc(const_ready, 1)

            def sums(f):
                residual_sum(f, 1)
                with pool.Fori(1, KC // 2) as i:
                    for c in range(2):
                        residual_sum(f, 2 * i + c)

            for m in range(1, KC):
                residual_sum(0, m)
            sums(1)
            sums(2)

            def head_squares(u0, c, n0, i=0):
                pool.wait_ge(unit_read, u0 + c + 2 * i + 1)
                ge(pool, z_fin, n0 + c + 2 * i - 1)
                pool.tensor_tensor(SQ[u0][c][0][:, :], KW[:, c], KW[:, c], ALU.mult).then_inc(z_sq, 1)

            for u0, n0 in ((U_K, 0), (U_Q, KC)):
                if u0 == U_Q:
                    pool.wait_ge(kv_stored, 48 * 2 * KC)
                head_squares(u0, 0, n0)
                head_squares(u0, 1, n0)
                with pool.Fori(1, KC // 2) as i:
                    for c in range(2):
                        head_squares(u0, c, n0, i)
            attention_pool()
            sums(3)

        @block.scalar
        def _(scalar):
            act.wait_ge(const_ready, 6)
            for t in range(NT):
                tok, rows = sides(t)
                for c in range(2):
                    n = AX_IN + 2 * t + c
                    act.wait_ge(aux_done, n + 1)
                    act.activation(ACC[:, 4 * c:4 * c + 4, tok:tok + rows],
                                   PS[:, 6 + n % 2, 0:4 * rows].rearrange("p (k r) -> p k r", r=rows),
                                   ACT.Copy).then_inc(aux_read, 1)
            act.wait_ge(aux_done, AX_VEC + 1)
            act.activation(vecs[:, :], PS[:, 6 + AX_VEC % 2, 0:N_VEC], ACT.Copy).then_inc(aux_read, 1)
            act.wait_ge(aux_done, AX_VEC + 2)
            act.activation(CST[:, :, :].rearrange("p k s -> p (k s)"),
                           PS[:, 6 + (AX_VEC + 1) % 2, 0:KC * DB * (CW - 1)], ACT.Copy).then_inc(aux_read, 1)
            act.wait_ge(aux_read, AX_VEC + 2)
            round_unit(0)
            residual_hi(0, 0, 0)
            round_unit(1)
            for m in range(1, KC):
                residual_hi(0, m, 0)
            rms_split_hi(0)

            def hid_hi_of(n, j):
                act.wait_ge(h_raw, n + 1)
                act.activation(HH[:, j], T1[:, :], ACT.Copy).then_inc(hid_hi, 1)

            def mixer(i, first=False):
                for m2 in range(2):
                    for j in range(3):
                        round_unit(3 * m2 + j + 2, i, 6)
                        if first and m2 == 0 and j == 0:
                            rms_root(0)
                    hid_hi_of(2 * i + m2, 2 * i + m2)

            mixer(0, True)
            with act.Fori(1, KC // 2) as i:
                mixer(i)

            def residual_turns(u0, split, f, turn=0, prefetch=True):
                def one(i, c):
                    round_unit(u0 + c + 2, turn + i)
                    act.wait_ge(unit_read, u0 + c + 2 * (turn + i) + 1)
                    residual_hi(split, c + 2 * i, f)
                one(0, 0)
                one(0, 1)
                with act.Fori(1, KC // 2) as i:
                    one(i, 0)
                    one(i, 1)

            for c in range(2):
                n = AX_CONV + c
                act.wait_ge(aux_done, n + 1)
                act.activation(CO[:, 512 * c:512 * c + 512], PS[0:(DB + 1) * (CW - 1), 6 + n % 2, :],
                               ACT.Copy).then_inc(aux_read, 1)
            act.wait_ge(gate_w_loaded, 16)
            act.activation(WFH[:, :, :], WFR[:, :, :], ACT.Copy).then_inc(gate_hi, 1)
            residual_turns(U_OUT, 1, 1)

            def mlp(l, s):
                U = U_MLP[l]
                rms_split_hi(s)

                def up(b, i, c, root=False):
                    round_unit(U + c + 2, KC * b + i)
                    if root:
                        rms_root(s)
                    hid_hi_of(HID[l] + KC * b + c + 2 * i, c + 2 * i)

                def down(b, i, c):
                    round_unit(U + KC + c + 2, KC * b + i)

                up(0, 0, 0, True)
                up(0, 0, 1)
                with act.Fori(1, KC // 2) as i:
                    up(0, i, 0)
                    up(0, i, 1)
                with act.Fori(0, KC // 2) as i:
                    down(0, i, 0)
                    down(0, i, 1)
                with act.Fori(1, FF_BLK - 1) as b:
                    with act.Fori(0, KC // 2) as i:
                        up(b, i, 0)
                        up(b, i, 1)
                    with act.Fori(0, KC // 2) as i:
                        down(b, i, 0)
                        down(b, i, 1)
                b = FF_BLK - 1
                with act.Fori(0, KC // 2) as i:
                    up(b, i, 0)
                    up(b, i, 1)
                if l == 0:
                    residual_turns(U + KC + 2 * KC * b, 2, 2)
                else:
                    with act.Fori(0, KC // 2 - 1) as i:
                        down(b, i, 0)
                        down(b, i, 1)

            mlp(0, 1)

            rms_split_hi(2)

            def head_hi(u0, c, n):
                act.wait_ge(z_sq, n + 1)
                ge(act, z_fin, n)
                act.activation(T2R[:, :], SQ[u0][c][0][:, :], ACT.Copy).then_inc(z_hi, 1)

            def head_root(n):
                for g in range(G):
                    act.wait_ge(aux_done, n[1] + g + 1)
                    act.activation(T2[:, g * GW:(g + 1) * GW], PS[:, 6 + (n[0] + g) % 2, 0:GW], ACT.Ln,
                                   scale=1.0 / HD, bias=epst[:, 0:1]).then_inc(aux_read, 1)
                act.wait_ge(aux_read, n[1] + G)
                act.activation(T2[:, 0:T], T2[:, 0:T], ACT.Exp, scale=-0.5).then_inc(z_inv, 1)

            def keep_k(i, c):
                m, n = c + 2 * i, ax(AX_K + G + 6 * c, 12, i)
                keep_tokens(n, m)
                store_tokens(n, out["k_prompt"], out["k_sample"], m)

            def copy_k(i, c):
                m = c + 2 * i
                act.wait_ge(z_fin, m + 1)
                act.activation(KS[:, m], KW[:, c % 2], ACT.Copy).then_inc(k_kept, 1)

            def keep_v(i, c):
                m, n = c + 2 * i, ax(AX_V + 3 * c, 6, i)
                keep_tokens(n, KC + m)
                store_tokens(n, out["v_prompt"], out["v_sample"], m)

            round_unit(U_K + 2)
            rms_root(2)
            for g in range(G):
                act.wait_ge(aux_done, AX_F + g + 1)
                act.activation(LF[:, g * GW:(g + 1) * GW], PS[0:NH, 6 + (AX_F + g) % 2, 0:GW],
                               ACT.Copy).then_inc(aux_read, 1)
            head_hi(U_K, 0, 0)
            head_root(ax(AX_K, 0, 0))
            round_unit(U_K + 3)
            head_hi(U_K, 1, 1)
            keep_k(0, 0)
            head_root(ax(AX_K + 6, 0, 0))
            copy_k(0, 0)
            with act.Fori(1, KC // 2) as i:
                round_unit(U_K + 2, i)
                head_hi(U_K, 0, 2 * i)
                keep_k(i - 1, 1)
                head_root(ax(AX_K, 12, i))
                copy_k(i - 1, 1)
                round_unit(U_K + 3, i)
                head_hi(U_K, 1, 2 * i + 1)
                keep_k(i, 0)
                head_root(ax(AX_K + 6, 12, i))
                copy_k(i, 0)
            round_unit(U_V + 2)
            keep_k(KC // 2 - 1, 1)
            copy_k(KC // 2 - 1, 1)
            keep_v(0, 0)
            round_unit(U_V + 3)
            act.wait_ge(gate_step, 3)
            act.activation(ZE[:, :], ZN[:, :], ACT.Exp).then_inc(gate_act, 1)
            act.wait_ge(gate_step, 4)
            act.activation(LF[:, :], ZU[:, :], ACT.Ln).then_inc(gate_act, 1)
            keep_v(0, 1)
            with act.Fori(1, KC // 2 - 1) as i:
                for c in range(2):
                    round_unit(U_V + c + 2, i)
                    keep_v(i, c)
            i = KC // 2 - 1
            round_unit(U_V + 2, i)
            keep_v(i, 0)
            round_unit(U_V + 3, i)
            act.wait_ge(unit_done, U_Q)
            with act.Fori(0, KC) as m:
                residual_hi(3, m)
            keep_v(i, 1)
            act.wait_ge(aux_done, AX_LF + 1)
            b = 6 + AX_LF % 2
            act.activation(LT[:, 0:NT - 1], PS[:, b, 0:NH * (NT - 1)].rearrange("p (t h) -> p t h", h=NH),
                           ACT.Copy).then_inc(lt_kept, 1)
            act.activation(LT[0:LAST, NT - 1], PS[0:LAST, b, NH * (NT - 1):NH * NT], ACT.Copy)\
               .then_inc(aux_read, 1)
            act.wait_ge(lt_kept, 1)
            act.wait_ge(aux_read, AX_LF + 1)
            full = P * (NT - 1)
            act.dma_start(out["logf_prompt"][0, 0:full].rearrange("(t p) h -> p t h", p=P), LT[:, 0:NT - 1])\
               .then_inc(logf_stored, 16)
            act.dma_start(out["logf_prompt"][0, full:NPR], LT[0:LASTP, NT - 1]).then_inc(logf_stored, 16)
            act.dma_start(out["logf_sample"].rearrange("b t h -> (b t) h"), LT[LASTP:LAST, NT - 1])\
               .then_inc(logf_stored, 16)
            act.wait_ge(gate_step, 9)
            act.dma_start(c_rows, C8[:, :]).then_inc(c_stored, 16)

            def q_turn(i):
                for c in range(2):
                    round_unit(U_Q + c + 2, i)
                    head_hi(U_Q, c, KC + c + 2 * i)
                    head_root(ax(AX_Q + 3 * c, 6, i))
            with act.Fori(0, KC // 2) as i:
                q_turn(i)

            attention_scalar()

            residual_turns(U_O, 4, 3)
            mlp(1, 3)
            y_scalar()

        @block.vector
        def _(vector):
            dve.memset(epst[:, :], EPS).then_inc(const_ready, 1)
            dve.memset(ones[:, :].bitcast(F32), 1.0).then_inc(const_ready, 1)
            dve.memset(heads1[:, :].bitcast(F32), 0.0).then_inc(heads_zero, 1)
            dve.wait_ge(heads_zero, 1)
            for h in range(2):
                s = slice(h * HD, (h + 1) * HD)
                dve.memset(heads1[s, s].bitcast(F32), 1.0).then_inc(const_ready, 1)
            cut_unit(0)
            residual_lo(0, 0)
            cut_unit(1)
            with dve.Fori(1, KC) as m:
                residual_lo(0, m)
            rms_split_lo(0)

            def scaled(c, i, stride, to, by):
                u = c + stride * i
                dve.wait_ge(unit_done, u + 1)
                dve.tensor_tensor(banks(to), result(c), banks(by), ALU.mult).then_inc(unit_read, 1)

            def hid_lo_of(n, j):
                dve.wait_ge(hid_hi, n + 1)
                dve.tensor_tensor(HL[:, j], T1[:, :], HH[:, j].bitcast(F32), ALU.subtract).then_inc(hid_lo, 1)

            T1P, T1S = T1[:, 0:NPR], T1[:, NPR:TOK].rearrange("p (b t) -> p b t", b=DB)
            RP, RS = R[:, 0:NPR], R[:, NPR:TOK].rearrange("p (b t) -> p b t", b=DB)

            def mixer(i, first=False):
                for m2 in range(2):
                    m, c = 2 * i + m2, 3 * m2
                    cut_unit(c + 2, i, 6)
                    if first and m2 == 0:
                        rms_inverse(0)
                    ge(dve, hid_lo, m)
                    scaled(c, i, 6, T1[:, :], R[:, :])
                    dve.wait_ge(unit_read, c + 6 * i + 1)
                    cut_unit(c + 3, i, 6)
                    scaled(c + 1, i, 6, T1[:, :], T1[:, :])
                    dve.wait_ge(unit_read, c + 1 + 6 * i + 1)
                    dve.tensor_tensor(UP[:, CW - 1:CW - 1 + NPR], T1P, RP, ALU.mult).then_inc(u_ready, 1)
                    dve.tensor_tensor(US[:, :, CW - 1:], T1S, RS, ALU.mult).then_inc(u_ready, 1)
                    dve.memset(UP[:, 0:CW - 1], 0.0).then_inc(u_ready, 1)
                    dve.tensor_copy(US[:, :, 0:CW - 1], CST[:, m].rearrange("p (b j) -> p b j", b=DB))\
                       .then_inc(u_ready, 1)
                    dve.wait_ge(u_ready, 4 * (m + 1))
                    dve.tensor_copy(UL[:, m, 0:CW - 1], UP[:, NPR:NPR + CW - 1]).then_inc(u_last, 1)
                    dve.tensor_copy(UL[:, m, CW - 1:].rearrange("p (b j) -> p b j", b=DB),
                                    US[:, :, DQ:DQ + CW - 1]).then_inc(u_last, 1)
                    for j in range(CW):
                        tap = vecs[:, bass.ds(G_CONV + KC * j + m, 1)]
                        src = ((T1P, UP[:, j:j + NPR]), (T1S, US[:, :, j:j + DQ]))
                        if j:
                            dve.wait_ge(conv_step, 2 * CW * m + 2 * j)
                        for to, x in src:
                            if j == 0:
                                dve.tensor_scalar(to, x, tap, None, ALU.mult).then_inc(conv_step, 1)
                            else:
                                dve.scalar_tensor_tensor(to, x, tap, to, ALU.mult, ALU.add)\
                                   .then_inc(conv_step, 1)
                    cut_unit(c + 4, i, 6)
                    dve.wait_ge(conv_step, 2 * CW * (m + 1))
                    scaled(c + 2, i, 6, T1[:, :], T1[:, :])
                    dve.wait_ge(unit_read, c + 2 + 6 * i + 1)
                    dve.tensor_tensor(T1[:, :], T1[:, :], R[:, :], ALU.mult).then_inc(h_raw, 1)
                    hid_lo_of(m, m)

            mixer(0, True)
            with dve.Fori(1, KC // 2) as i:
                mixer(i)

            dve.wait_ge(gate_hi, 1)
            dve.tensor_tensor(WFL[:, :, :], WFR[:, :, :], WFH[:, :, :].bitcast(F32), ALU.subtract)\
               .then_inc(gate_lo, 1)

            def add_residual(c, i, m):
                u = c + 2 * i
                dve.wait_ge(unit_done, u + 1)
                dve.tensor_tensor(banks(ACC[:, m]), result(c), banks(ACC[:, m]), ALU.add).then_inc(unit_read, 1)

            def residual_turns(u0, split):
                with dve.Fori(0, KC // 2) as i:
                    for c in range(2):
                        cut_unit(u0 + c + 2, i)
                        add_residual(u0 + c, i, c + 2 * i)
                        residual_lo(split, c + 2 * i)

            residual_turns(U_OUT, 1)

            def mlp(l, s):
                U = U_MLP[l]
                rms_split_lo(s)

                def up(b, i, c, inverse=False):
                    n, u = HID[l] + KC * b + c + 2 * i, U + c + 2 * (KC * b + i)
                    cut_unit(U + c + 2, KC * b + i)
                    if inverse:
                        rms_inverse(s)
                    dve.wait_ge(hid_lo, n)
                    dve.wait_ge(unit_done, u + 1)
                    dve.scalar_tensor_tensor(banks(T1[:, :]), result(c), 0.0, banks(R[:, :]), ALU.max,
                                             ALU.mult).then_inc(unit_read, 1)
                    dve.wait_ge(unit_read, u + 1)
                    dve.tensor_tensor(T1[:, :], T1[:, :], T1[:, :], ALU.mult).then_inc(h_raw, 1)
                    hid_lo_of(n, c + 2 * i)

                def down(b, i, c):
                    cut_unit(U + KC + c + 2, KC * b + i)
                    add_residual(U + KC + c, KC * b + i, c + 2 * i)

                up(0, 0, 0, True)
                up(0, 0, 1)
                with dve.Fori(1, KC // 2) as i:
                    up(0, i, 0)
                    up(0, i, 1)
                with dve.Fori(0, KC // 2) as i:
                    down(0, i, 0)
                    down(0, i, 1)
                with dve.Fori(1, FF_BLK - 1) as b:
                    with dve.Fori(0, KC // 2) as i:
                        up(b, i, 0)
                        up(b, i, 1)
                    with dve.Fori(0, KC // 2) as i:
                        down(b, i, 0)
                        down(b, i, 1)
                b = FF_BLK - 1
                with dve.Fori(0, KC // 2) as i:
                    up(b, i, 0)
                    up(b, i, 1)
                if l == 0:
                    residual_turns(U + KC + 2 * KC * b, 2)
                else:
                    with dve.Fori(0, KC // 2 - 1) as i:
                        down(b, i, 0)
                        down(b, i, 1)
                    down(b, KC // 2 - 1, 0)
                    down(b, KC // 2 - 1, 1)

            mlp(0, 1)

            rms_split_lo(2)

            def head_lo(u0, n, par):
                dve.wait_ge(z_hi, n + 1)
                dve.tensor_tensor(SQ[u0][par][1][:, :], SQ[u0][par][0][:, :], T2R[:, :].bitcast(F32), ALU.subtract)\
                   .then_inc(z_lo, 1)

            def head_fin(n, par, gain, to):
                dve.wait_ge(z_inv, n + 1)
                dve.scalar_tensor_tensor(to, KW[:, par], vecs[:, gain:gain + 1], T2[:, 0:T],
                                         ALU.mult, ALU.mult).then_inc(z_fin, 1)

            def k_turn(i, c, inverse=False, first=False):
                if first:
                    cut_unit(U_K + c + 2, i)
                if inverse:
                    rms_inverse(2)
                    dve.wait_ge(conv_stored, 32)
                if not first:
                    dve.wait_ge(aux_read, AX_K + 3 + 6 * (c - 2) + 12 * i + G)
                    dve.wait_ge(k_kept, c + 2 * i - 1)
                scaled(U_K + c, i, 2, KW[:, c], R[:, :])
                if c or not first:
                    head_fin(c + 2 * i - 1, 1 - c, G_KN, KW[:, 1 - c])
                if not first:
                    cut_unit(U_K + c + 2, i)
                head_lo(U_K, c + 2 * i, c)

            k_turn(0, 0, True, True)
            k_turn(0, 1, False, True)
            with dve.Fori(1, KC // 2) as i:
                k_turn(i, 0)
                k_turn(i, 1)
            for c in range(2):
                cut_unit(U_V + c + 2)
                if c == 0:
                    head_fin(KC - 1, 1, G_KN, KW[:, 1])
                dve.wait_ge(aux_read, AX_K + 3 + 6 * (KC - 2 + c) + G)
                dve.wait_ge(k_kept, KC - 1 + c)
                scaled(U_V + c, 0, 2, KW[:, c], R[:, :])
            dve.wait_ge(bf_loaded, 16)
            dve.wait_ge(aux_read, AX_F + G)
            dve.tensor_tensor(Z[:, :], LF[:, :], R[0:NH, :], ALU.mult).then_inc(gate_step, 1)
            dve.wait_ge(gate_step, 1)
            dve.tensor_scalar(Z[:, :], Z[:, :], BF[:, 0:1], None, ALU.add).then_inc(gate_step, 1)
            dve.wait_ge(gate_step, 2)
            dve.scalar_tensor_tensor(ZN[:, :], Z[:, :], -1.0, Z[:, :], ALU.mult, ALU.min).then_inc(gate_step, 1)
            dve.wait_ge(gate_act, 1)
            dve.tensor_scalar(ZU[:, :], ZE[:, :], 1.0, None, ALU.add).then_inc(gate_step, 1)
            dve.wait_ge(gate_act, 2)
            dve.scalar_tensor_tensor(ZU[:, :], ZU[:, :], 1.0, ZE[:, :], ALU.subtract, ALU.subtract)\
               .then_inc(gate_step, 1)
            dve.wait_ge(gate_step, 5)
            dve.tensor_tensor(LF[:, :], LF[:, :], ZU[:, :], ALU.subtract).then_inc(gate_step, 1)
            dve.wait_ge(gate_step, 6)
            dve.scalar_tensor_tensor(LF[:, :], Z[:, :], 0.0, LF[:, :], ALU.min, ALU.subtract).then_inc(gate_step, 1)
            dve.wait_ge(gate_step, 7)
            dve.tensor_tensor_scan(C8[:, :], ones[0:NH, 0:1].bitcast(F32).to_broadcast([NH, NPR]), LF[:, 0:NPR],
                                   0.0, ALU.mult, ALU.add).then_inc(gate_step, 1)
            dve.wait_ge(gate_step, 8)
            dve.tensor_scalar(C8[:, :], C8[:, :], -1.0 / SCALE, None, ALU.mult).then_inc(gate_step, 1)
            with dve.Fori(1, KC // 2) as i:
                for c in range(2):
                    cut_unit(U_V + c + 2, i)
                    dve.wait_ge(aux_read, AX_V + 3 * (c - 2) + 6 * i + G)
                    scaled(U_V + c, i, 2, KW[:, c], R[:, :])
            dve.wait_ge(unit_done, U_Q)
            with dve.Fori(0, KC) as m:
                residual_lo(3, m)

            def q_turn(i, c, first=False):
                if first:
                    cut_unit(U_Q + c + 2, i)
                    dve.wait_ge(aux_read, AX_V + 3 * KC)
                scaled(U_Q + c, i, 2, KW[:, c], R[:, :])
                if c or not first:
                    head_fin(KC + c + 2 * i - 1, 1 - c, G_QN, QS[:, c + 2 * i - 1])
                if not first:
                    cut_unit(U_Q + c + 2, i)
                head_lo(U_Q, KC + c + 2 * i, c)

            q_turn(0, 0, True)
            q_turn(0, 1, True)
            dve.wait_ge(logf_stored, 48)
            dve.wait_ge(c_stored, 16)
            with dve.Fori(1, KC // 2) as i:
                q_turn(i, 0)
                q_turn(i, 1)
            head_fin(2 * KC - 1, 1, G_QN, QS[:, KC - 1])

            attention_vector()

            residual_turns(U_O, 4)
            mlp(1, 3)
            y_vector()

        @block.tensor
        def _(tensor):
            pe.wait_ge(const_ready, 6)
            for t in range(NT):
                tok, rows = sides(t)
                pe.wait_ge(in_loaded[t], 16 if 0 < t < NT - 1 else 32)
                for c in range(2):
                    n = AX_IN + 2 * t + c
                    ge(pe, aux_read, n - 1)
                    for k in range(4):
                        mm = pe.transpose(PS[:, 6 + n % 2, k * rows:(k + 1) * rows],
                                          IN[0:rows, t, P * (4 * c + k):P * (4 * c + k + 1)],
                                          ident[0:rows, 0:rows])
                    mm.then_inc(aux_done, 1)
            pe.wait_ge(vec_loaded, 16 * 8)
            pe.wait_ge(aux_read, AX_VEC - 1)
            pe.transpose(PS[:, 6 + AX_VEC % 2, 0:N_VEC], VIN[:, :], ident[0:N_VEC, 0:N_VEC]).then_inc(aux_done, 1)
            pe.wait_ge(state_loaded, 16)
            pe.wait_ge(aux_read, AX_VEC)
            ns = DB * (CW - 1)
            for k in range(KC):
                mm = pe.transpose(PS[:, 6 + (AX_VEC + 1) % 2, k * ns:(k + 1) * ns], STI[:, P * k:P * (k + 1)],
                                  ident[0:ns, 0:ns])
            mm.then_inc(aux_done, 1)

            def mixer(i, first=False):
                for c in range(6):
                    unit(c, i, 6, ready=x_ready(0) if first and c == 0 else None)
                    if first and c == 0:
                        rms_sums(0)

            mixer(0, True)
            with pe.Fori(1, KC // 2) as i:
                mixer(i)

            def eight(u0, turn=0, hi=XH, lo=XL, ready=None, after=None, short=False):
                unit(u0, turn, 2, hi, lo, ready)
                if after:
                    after()
                unit(u0 + 1, turn, 2, hi, lo)
                with pe.Fori(1, KC // 2 - short) as i:
                    unit(u0, turn + i, 2, hi, lo)
                    unit(u0 + 1, turn + i, 2, hi, lo)
                if short:
                    unit(u0, turn + KC // 2 - 1, 2, hi, lo)

            def hid_ready(n):
                return lambda k: pe.wait_ge(hid_lo, n + k + 1)

            pe.wait_ge(u_last, 2 * KC)
            for c in range(2):
                n = AX_CONV + c
                pe.wait_ge(aux_read, n - 1)
                for k in range(4):
                    mm = pe.transpose(PS[0:(DB + 1) * (CW - 1), 6 + n % 2, P * k:P * (k + 1)],
                                      UL[:, 4 * c + k, :], ident[:, :])
                mm.then_inc(aux_done, 1)
            eight(U_OUT, 0, HH, HL, hid_ready(0))

            def mlp(l, split, s):
                U = U_MLP[l]
                eight(U, 0, XH, XL, x_ready(split), lambda: rms_sums(s))
                eight(U + KC, 0, HH, HL, hid_ready(HID[l]))
                with pe.Fori(1, FF_BLK - 1) as b:
                    eight(U, KC * b)
                    eight(U + KC, KC * b, HH, HL, hid_ready(HID[l] + KC * b))
                b = FF_BLK - 1
                eight(U, KC * b)
                eight(U + KC, KC * b, HH, HL, hid_ready(HID[l] + KC * b), short=(l == 1))

            mlp(0, 1, 1)

            def head_sums(u0, c, n, z):
                def f(groups):
                    return lambda: column_sums(n, heads1, lambda: pe.wait_ge(z_lo, z + 1), SQ[u0][c][1], groups)
                return {6: f((0, 1)), 7: f((2,))}

            def turn_k(i, c):
                def f(groups):
                    def g():
                        if 0 in groups:
                            pe.wait_ge(z_fin, c + 2 * i + 1)
                        turn_tokens(c % 2, ax(AX_K + G + 6 * c, 12, i), groups)
                    return g
                return {4: f((0, 1)), 5: f((2,))}

            def turn_v(i, c, at=4):
                def f(groups):
                    def g():
                        if 0 in groups:
                            pe.wait_ge(unit_read, U_V + c + 2 * i + 1)
                        turn_tokens(c % 2, ax(AX_V + 3 * c, 6, i), groups)
                    return g
                return {at: f((0, 1)), at + 1: f((2,))}

            unit(U_K, ready=x_ready(2))
            rms_sums(2)
            pe.wait_ge(gate_lo, 1)
            for g in range(G):
                n = AX_F + g
                pe.wait_ge(aux_read, n - 1)
                for k in range(KC):
                    for j, (w, x) in enumerate(((WFH, XH), (WFH, XL), (WFL, XH))):
                        mm = pe.matmul(PS[0:NH, 6 + n % 2, 0:GW], w[:, k], x[:, k, g * GW:(g + 1) * GW],
                                       start=(k == 0 and j == 0), stop=(k == KC - 1 and j == 2))
                mm.then_inc(aux_done, 1)
            unit(U_K + 1, mid=head_sums(U_K, 0, ax(AX_K, 0, 0), 0))
            with pe.Fori(1, KC // 2) as i:
                unit(U_K, i, mid={**turn_k(i - 1, 0), **head_sums(U_K, 1, ax(AX_K - 6, 12, i), 2 * i - 1)})
                unit(U_K + 1, i, mid={**turn_k(i - 1, 1), **head_sums(U_K, 0, ax(AX_K, 12, i), 2 * i)})
            last = KC // 2 - 1
            unit(U_V, mid={**turn_k(last, 0), **head_sums(U_K, 1, ax(AX_K + 6 * (KC - 1), 0, 0), KC - 1)})
            unit(U_V + 1, mid={**turn_k(last, 1), **turn_v(0, 0, 6)})
            with pe.Fori(1, KC // 2) as i:
                unit(U_V, i, mid=turn_v(i - 1, 1))
                unit(U_V + 1, i, mid=turn_v(i, 0))

            def turn_logf():
                pe.wait_ge(gate_step, 7)
                pe.wait_ge(aux_read, AX_LF - 1)
                for t in range(NT):
                    tok, rows = sides(t)
                    mm = pe.transpose(PS[0:rows, 6 + AX_LF % 2, NH * t:NH * t + NH], LF[:, tok:tok + rows],
                                      ident[0:NH, 0:NH])
                mm.then_inc(aux_done, 1)

            unit(U_Q, ready=x_ready(3), mid={**turn_v(last, 1), 6: turn_logf})
            unit(U_Q + 1, mid=head_sums(U_Q, 0, ax(AX_Q, 0, 0), KC))
            with pe.Fori(1, KC // 2) as i:
                unit(U_Q, i, mid=head_sums(U_Q, 1, ax(AX_Q - 3, 6, i), KC + 2 * i - 1))
                unit(U_Q + 1, i, mid=head_sums(U_Q, 0, ax(AX_Q, 6, i), KC + 2 * i))
            for f in head_sums(U_Q, 1, ax(AX_Q + 3 * (KC - 1), 0, 0), 2 * KC - 1).values():
                f()

            attention_tensor()

            eight(U_O, 0, HH, HL, o_ready)
            mlp(1, 4, 3)
            y_tensor()


_OUTS = (("y_prompt", (1, SEQ, D)), ("y_sample", (DB, DQ, D)), ("k_prompt", (1, NPR, NH, HD)),
         ("v_prompt", (1, NPR, NH, HD)), ("logf_prompt", (1, NPR, NH)), ("conv_prompt", (1, 1, CW - 1, D)),
         ("k_sample", (DB, DQ, NH, HD)), ("v_sample", (DB, DQ, NH, HD)), ("logf_sample", (DB, DQ, NH)),
         ("conv_sample", (1, DB, CW - 1, D)))


def kernel(**inputs):
    import concourse.bacc as bacc
    from concourse.bass_utils import run_bass_kernel_spmd

    nc = bacc.Bacc("TRN2", target_bir_lowering=False, num_devices=1, dynamic_dma_scratch_size=64)
    arrays, ins, outs = {}, {}, {}
    for name, x in inputs.items():
        x = np.ascontiguousarray(x)
        arrays["in_" + name] = x
        ins[name] = nc.dram_tensor("in_" + name, x.shape, mybir.dt.from_np(x.dtype), kind="ExternalInput").ap()
    for name, shape in _OUTS:
        outs[name] = nc.dram_tensor("out_" + name, shape, F32, kind="ExternalOutput").ap()
    trunk(nc, ins, outs)
    r = run_bass_kernel_spmd(nc, [arrays], core_ids=[0])
    return tuple(r.results[0]["out_" + name] for name, _ in _OUTS)
```
